# Optimizing a Trainium2 kernel written in Bass

```python
import math
import jax, jax.numpy as jnp
from jax import lax
import numpy as np

D_MODEL = 1024
BATCH = 1
SEQ = 256
DEPTH = 2

GRID_W = 64
CTX_LEN = 256
N_MIXERS = 2
N_SUB = 3
D_FF = 2816
MACARON_W = 0.5
NORM_EPS = 1e-6
GDN_DK = 128
GDN_DV = 128
GDN_HEADS = D_MODEL // GDN_DV
GDN_CONV = 5
GDN_CHUNK = 64
GDN_IN = 4 * D_MODEL + 4 * GDN_HEADS
DIFF_HD = 64
DIFF_VD = 2 * DIFF_HD
DIFF_HEADS = D_MODEL // DIFF_VD
DIFF_IN = 3 * D_MODEL
Q_BLOCK = 128
ROPE_BASE = 10000.0
N_GDN = (DEPTH + 1) // 2
N_DIFF = DEPTH // 2

kernel_name = 'hybrid_gdn_diffattn_macaron_dit'

F32 = jnp.float32

def rmsnorm(x, gain):
    xf = x.astype(F32)
    y = xf * lax.rsqrt(jnp.mean(xf * xf, axis=-1, keepdims=True) + NORM_EPS)
    return (y * gain.astype(F32)).astype(x.dtype)

def l2norm(x):
    xf = x.astype(F32)
    return xf * lax.rsqrt(jnp.sum(xf * xf, axis=-1, keepdims=True) + NORM_EPS)

def modulation(cvec, w, b):
    m = jax.nn.silu(cvec) @ w + b
    return m.reshape(cvec.shape[0], N_SUB, 3, 1, D_MODEL).transpose(1, 2, 0, 3, 4)

def pre(x, mod_j, gain):
    shift, scale, _ = mod_j
    return rmsnorm(x, gain) * (1 + scale) + shift

def swiglu(h, w_in, w_out):
    g, u = jnp.split(h @ w_in, 2, axis=-1)
    return (jax.nn.silu(g) * u) @ w_out

def ffn_sublayer(x, mod_j, g_pre, g_post, w_in, w_out):
    h = pre(x, mod_j, g_pre)
    return x + MACARON_W * mod_j[2] * rmsnorm(swiglu(h, w_in, w_out), g_post)

def short_conv(x, w):
    ch = x.shape[-1]
    return lax.conv_general_dilated(x, w[:, None, :].astype(x.dtype), window_strides=(1,),
                                    padding=[(GDN_CONV // 2, GDN_CONV // 2)],
                                    dimension_numbers=('NWC', 'WIO', 'NWC'),
                                    feature_group_count=ch)

def gated_delta_scan(q, k, v, logdecay, beta, S0, with_out):
    B_, T, H, _ = q.shape
    C = GDN_CHUNK
    N = T // C

    def chunks(a):
        a = a.astype(F32).reshape((B_, N, C, H) + a.shape[3:])
        return jnp.moveaxis(a, (1, 3), (0, 2))

    qc, kc, vc, gc, bc = map(chunks, (q, k, v, logdecay, beta))
    G = jnp.cumsum(gc, axis=-1)
    idx = jnp.arange(C)
    incl = idx[:, None] >= idx[None, :]
    strict = idx[:, None] > idx[None, :]
    Gamma = jnp.exp(jnp.where(incl, G[..., :, None] - G[..., None, :], -jnp.inf))
    kb = kc * bc[..., None]
    A = jnp.where(strict, jnp.einsum('nbhcd,nbhsd->nbhcs', kb, kc) * Gamma, 0.0)
    eye = jnp.eye(C, dtype=F32)
    Tinv = lax.linalg.triangular_solve(eye + A, jnp.broadcast_to(eye, A.shape), left_side=True,
                                       lower=True, unit_diagonal=True)
    u = jnp.einsum('nbhcs,nbhse->nbhce', Tinv, vc * bc[..., None])
    w = jnp.einsum('nbhcs,nbhsd->nbhcd', Tinv, kb * jnp.exp(G)[..., None])
    G_last = G[..., -1]
    k_tail = kc * jnp.exp(G_last[..., None] - G)[..., None]
    xs = (u, w, k_tail, G_last)
    if with_out:
        q_dec = qc * jnp.exp(G)[..., None]
        intra = jnp.einsum('nbhcd,nbhsd->nbhcs', qc, kc) * Gamma
        xs = xs + (q_dec, intra)

    def step(S, xs_n):
        u_n, w_n, kt_n, gl_n = xs_n[:4]
        v_new = u_n - jnp.einsum('bhcd,bhde->bhce', w_n, S)
        S_next = S * jnp.exp(gl_n)[..., None, None] + jnp.einsum('bhcd,bhce->bhde', kt_n, v_new)
        if with_out:
            qd_n, in_n = xs_n[4:]
            o = jnp.einsum('bhcd,bhde->bhce', qd_n, S) + jnp.einsum('bhcs,bhse->bhce', in_n, v_new)
            return S_next, o
        return S_next, None

    S_fin, o = lax.scan(step, S0.astype(F32), xs)
    if with_out:
        o = jnp.moveaxis(o, (0, 2), (1, 3)).reshape(B_, T, H, v.shape[-1])
    return o, S_fin

def gdn_project(x, w_in, conv_w, A_log, dt_bias):
    B_, T = x.shape[:2]
    p = x @ w_in
    qkv, gate, a, b = jnp.split(p, [3 * D_MODEL, 4 * D_MODEL, 4 * D_MODEL + 2 * GDN_HEADS], axis=-1)
    qkv = jax.nn.silu(short_conv(qkv, conv_w))
    q, k, v = jnp.split(qkv, 3, axis=-1)
    q = l2norm(q.reshape(B_, T, GDN_HEADS, GDN_DK)) * (GDN_DK ** -0.5)
    k = l2norm(k.reshape(B_, T, GDN_HEADS, GDN_DK))
    v = v.reshape(B_, T, GDN_HEADS, GDN_DV)
    a = a.astype(F32).reshape(B_, T, 2, GDN_HEADS)
    b = b.astype(F32).reshape(B_, T, 2, GDN_HEADS)
    logdecay = -jnp.exp(A_log.astype(F32)) * jax.nn.softplus(a + dt_bias.astype(F32))
    beta = jax.nn.sigmoid(b)
    return q, k, v, gate, logdecay, beta

def gdn_out(o, gate, o_gain, w_out, dtype):
    B_, T = o.shape[:2]
    y = rmsnorm(o, o_gain) * jax.nn.silu(gate.astype(F32)).reshape(o.shape)
    return y.reshape(B_, T, D_MODEL).astype(dtype) @ w_out

def gdn_mixer(hl, hc, w_in, conv_w, A_log, dt_bias, o_gain, w_out, with_ctx_out):
    ql, kl, vl, gl, dl, bl = gdn_project(hl, w_in, conv_w, A_log, dt_bias)
    qc, kc, vc, gc, dc, bc = gdn_project(hc, w_in, conv_w, A_log, dt_bias)
    S0 = jnp.zeros((hl.shape[0], GDN_HEADS, GDN_DK, GDN_DV), F32)
    outs_l, outs_c = [], []
    for d in range(2):
        rev = (lambda a: a[:, ::-1]) if d == 1 else (lambda a: a)
        oc, Sc = gated_delta_scan(rev(qc), rev(kc), rev(vc), rev(dc[:, :, d]), rev(bc[:, :, d]), S0, with_ctx_out)
        ol, _ = gated_delta_scan(rev(ql), rev(kl), rev(vl), rev(dl[:, :, d]), rev(bl[:, :, d]), Sc, True)
        outs_l.append(rev(ol))
        if with_ctx_out:
            outs_c.append(rev(oc))
    yl = gdn_out(outs_l[0] + outs_l[1], gl, o_gain, w_out, hl.dtype)
    yc = gdn_out(outs_c[0] + outs_c[1], gc, o_gain, w_out, hc.dtype) if with_ctx_out else None
    return yl, yc

def axial_rope(row, col):
    half = DIFF_HD // 2
    inv = ROPE_BASE ** (-jnp.arange(0, half, 2, dtype=F32) / half)
    ang = jnp.concatenate([row[:, None].astype(F32) * inv, col[:, None].astype(F32) * inv], axis=-1)
    return jnp.cos(ang), jnp.sin(ang)

def apply_rope(x, cos, sin):
    xf = x.astype(F32)
    x1, x2 = xf[..., 0::2], xf[..., 1::2]
    c = cos[None, :, None, None, :]
    s = sin[None, :, None, None, :]
    return jnp.stack([x1 * c - x2 * s, x1 * s + x2 * c], axis=-1).reshape(x.shape).astype(x.dtype)

def diff_attend(qb, keys, vals, lam):
    s = jnp.einsum('bqhmd,bkhmd->bhmqk', qb, keys).astype(F32) * (DIFF_HD ** -0.5)
    p = jax.nn.softmax(s, axis=-1)
    a = p[:, :, 0] - lam * p[:, :, 1]
    return jnp.einsum('bhqk,bkhe->bqhe', a.astype(vals.dtype), vals)

def diff_out(o, subln, lam_init, w_out):
    B_, T = o.shape[:2]
    y = rmsnorm(o, subln) * (1.0 - lam_init)
    return y.reshape(B_, T, D_MODEL) @ w_out

def diff_mixer(hl, hc, w_in, lam_p, subln, w_out, lam_init, cos, sin, with_ctx_out):
    def project(x):
        B_, T = x.shape[:2]
        q, k, v = jnp.split(x @ w_in, 3, axis=-1)
        return (q.reshape(B_, T, DIFF_HEADS, 2, DIFF_HD), k.reshape(B_, T, DIFF_HEADS, 2, DIFF_HD),
                v.reshape(B_, T, DIFF_HEADS, DIFF_VD))
    ql, kl, vl = project(hl)
    qc, kc, vc = project(hc)
    ql, kl = apply_rope(ql, cos, sin), apply_rope(kl, cos, sin)
    lp = lam_p.astype(F32)
    lam = jnp.exp(jnp.sum(lp[0] * lp[1])) - jnp.exp(jnp.sum(lp[2] * lp[3])) + lam_init
    keys = jnp.concatenate([kc, kl], axis=1)
    vals = jnp.concatenate([vc, vl], axis=1)
    B_, T = hl.shape[:2]
    nb = T // Q_BLOCK
    qblocks = ql.reshape(B_, nb, Q_BLOCK, DIFF_HEADS, 2, DIFF_HD).transpose(1, 0, 2, 3, 4, 5)
    ol = lax.map(lambda qb: diff_attend(qb, keys, vals, lam), qblocks)
    ol = ol.transpose(1, 0, 2, 3, 4).reshape(B_, T, DIFF_HEADS, DIFF_VD)
    yl = diff_out(ol, subln, lam_init, w_out)
    yc = diff_out(diff_attend(qc, kc, vc, lam), subln, lam_init, w_out) if with_ctx_out else None
    return yl, yc

def setup_inputs(seed: int = 0) -> dict:
    key = jax.random.key(seed)
    ks = jax.random.split(key, 24)
    nrm = jax.random.normal
    D = D_MODEL
    dt = jnp.exp(jax.random.uniform(ks[12], (N_GDN, 2, GDN_HEADS), F32, math.log(1e-3), math.log(1e-1)))
    return {
        'x': nrm(ks[0], (BATCH, SEQ, D), F32),
        'c': nrm(ks[1], (BATCH, D), F32),
        'ctx': nrm(ks[2], (BATCH, CTX_LEN, D), F32),
        'c_ctx': nrm(ks[3], (D,), F32),
        'w_mod': nrm(ks[4], (DEPTH, D, N_SUB * 3 * D), F32) * (0.5 * D ** -0.5),
        'b_mod': nrm(ks[5], (DEPTH, N_SUB * 3 * D), F32) * 0.02,
        'norm_pre': 1.0 + 0.02 * nrm(ks[6], (DEPTH, N_SUB, D), F32),
        'norm_post': 1.0 + 0.02 * nrm(ks[7], (DEPTH, N_SUB, D), F32),
        'ffn_w_in': nrm(ks[8], (DEPTH, 2, D, 2 * D_FF), F32) * D ** -0.5,
        'ffn_w_out': nrm(ks[9], (DEPTH, 2, D_FF, D), F32) * D_FF ** -0.5,
        'gdn_w_in': nrm(ks[10], (N_GDN, D, GDN_IN), F32) * D ** -0.5,
        'gdn_conv': nrm(ks[11], (N_GDN, GDN_CONV, 3 * D), F32) * GDN_CONV ** -0.5,
        'gdn_A_log': jnp.log(jax.random.uniform(ks[13], (N_GDN, 2, GDN_HEADS), F32, 1.0, 16.0)),
        'gdn_dt_bias': dt + jnp.log(-jnp.expm1(-dt)),
        'gdn_o_gain': 1.0 + 0.02 * nrm(ks[14], (N_GDN, GDN_DV), F32),
        'gdn_w_out': nrm(ks[15], (N_GDN, D, D), F32) * D ** -0.5,
        'diff_w_in': nrm(ks[16], (N_DIFF, D, DIFF_IN), F32) * D ** -0.5,
        'diff_lambda': nrm(ks[17], (N_DIFF, 4, DIFF_HD), F32) * 0.1,
        'diff_subln': 1.0 + 0.02 * nrm(ks[18], (N_DIFF, DIFF_VD), F32),
        'diff_w_out': nrm(ks[19], (N_DIFF, D, D), F32) * D ** -0.5,
    }

def reference(x, c, ctx, c_ctx, w_mod, b_mod, norm_pre, norm_post, ffn_w_in, ffn_w_out,
              gdn_w_in, gdn_conv, gdn_A_log, gdn_dt_bias, gdn_o_gain, gdn_w_out,
              diff_w_in, diff_lambda, diff_subln, diff_w_out):
    T = x.shape[1]
    ROWS = T // GRID_W
    row = jnp.repeat(jnp.arange(ROWS), GRID_W)
    col = jnp.tile(jnp.arange(GRID_W), ROWS)
    cos, sin = axial_rope(row, col)
    xl, xc = x, ctx
    for l in range(DEPTH):
        last = l == DEPTH - 1
        mod_l = modulation(c, w_mod[l], b_mod[l])
        mod_c = modulation(c_ctx[None], w_mod[l], b_mod[l])
        xl = ffn_sublayer(xl, mod_l[0], norm_pre[l, 0], norm_post[l, 0], ffn_w_in[l, 0], ffn_w_out[l, 0])
        xc = ffn_sublayer(xc, mod_c[0], norm_pre[l, 0], norm_post[l, 0], ffn_w_in[l, 0], ffn_w_out[l, 0])
        hl = pre(xl, mod_l[1], norm_pre[l, 1])
        hc = pre(xc, mod_c[1], norm_pre[l, 1])
        i = l // N_MIXERS
        if l % N_MIXERS == 0:
            yl, yc = gdn_mixer(hl, hc, gdn_w_in[i], gdn_conv[i], gdn_A_log[i], gdn_dt_bias[i],
                               gdn_o_gain[i], gdn_w_out[i], not last)
        else:
            lam_init = 0.8 - 0.6 * math.exp(-0.3 * l)
            yl, yc = diff_mixer(hl, hc, diff_w_in[i], diff_lambda[i], diff_subln[i], diff_w_out[i],
                                lam_init, cos, sin, not last)
        xl = xl + mod_l[1][2] * rmsnorm(yl, norm_post[l, 1])
        if not last:
            xc = xc + mod_c[1][2] * rmsnorm(yc, norm_post[l, 1])
            xc = ffn_sublayer(xc, mod_c[2], norm_pre[l, 2], norm_post[l, 2], ffn_w_in[l, 1], ffn_w_out[l, 1])
        xl = ffn_sublayer(xl, mod_l[2], norm_pre[l, 2], norm_post[l, 2], ffn_w_in[l, 1], ffn_w_out[l, 1])
    return xl


_drawn_inputs = setup_inputs


def setup_inputs(seed=0):
    import zlib

    import numpy as np

    out = dict(_drawn_inputs(seed))
    spreads = {}
    factors = {'norm_pre': 4.066,
     'norm_post': 5.508,
     'gdn_o_gain': 8.0,
     'diff_lambda': 5.719,
     'diff_subln': 8.0}
    for name, (base, spread) in spreads.items():
        noise = np.random.default_rng([zlib.crc32(name.encode()), seed]).standard_normal(out[name].shape)
        drawn = base * np.exp(spread * noise) if base else spread * noise
        out[name] = __import__('jax').numpy.asarray(drawn.astype(out[name].dtype))
    for name, factor in factors.items():
        out[name] = (out[name] * factor).astype(out[name].dtype)
    return out
```

```python
import math
from contextlib import ExitStack, contextmanager

import numpy as np

import concourse.bass as bass
from concourse import mybir

F32 = mybir.dt.float32
ALU = mybir.AluOpType
ACT = mybir.ActivationFunctionType
AX_X = mybir.AxisListType.X
ds = bass.ds

P = 128
D = 1024
KC = D // P
LAT = 256
CTX = 256
TOK = CTX + LAT
DFF = 2816
FC = DFF // P
DEPTH = 2
NSUB = 3
HEADS = 8
TAPS = 5
PAD = TAPS // 2
GRID_W = 64
HALF = 64
NC = TOK // P
EPS = 1e-6
GDN_IN = 4 * D + 4 * HEADS
LAM_INIT = 0.8 - 0.6 * math.exp(-0.3)
LEVELS = [2, 4, 8, 16, 32, 64]
WALK = [[0, 1, 2, 3], [1, 0, 3, 2]]

N_SMALL = 9
SLOTS = 4
UNIT = FC * P
MSLOTS = 4
MVEC = DEPTH * NSUB * 3

ROWS = {"norms": 96, "conv": 3 * KC * TAPS, "b_mod0": 72, "b_mod1": 72, "cond": 18}

SUBS = [("ffn", 0, 0), ("gdn", 0, 1), ("ffn", 0, 2), ("ffn", 1, 0), ("diff", 1, 1), ("ffn", 1, 2)]
UNITS = {"ffn": FC + KC, "gdn": 16 + 1 + 4, "diff": 12 + 4}
GROUPS = {"ffn": 2 * FC + KC, "gdn": 4 * KC + 1 + KC, "diff": 2 * KC + 16 + KC}
MOD_FIRST = 24
MOD_INSIDE = {0: 48, 2: 48, 3: 24}


def constant_blocks():
    i = np.arange(P)
    s, c = i[:, None], i[None, :]
    blocks = {"ident": (s == c), "ones": np.ones((P, P))}
    blocks["incl0"], blocks["incl1"] = s <= c, s >= c
    blocks["strict0"], blocks["strict1"] = s < c, s > c
    pair = (s // 2 == c // 2)
    blocks["pair0"] = -1.0 * (pair & (s < c))
    blocks["pair1"] = -1.0 * (pair & (s > c))
    for w in LEVELS:
        same = (s // (2 * w)) == (c // (2 * w))
        blocks[f"lev0_{w}"] = same & (s % (2 * w) >= w) & (c % (2 * w) < w)
        blocks[f"lev1_{w}"] = same & (s % (2 * w) < w) & (c % (2 * w) >= w)
    rot = np.zeros((P, P))
    for k in range(0, P, 2):
        rot[k + 1, k] = -1.0
        rot[k, k + 1] = 1.0
    blocks["rot"] = rot
    half = HALF // 2
    inv = (np.float32(10000.0) ** (-np.arange(0, half, 2, dtype=np.float32) / np.float32(half))).astype(np.float32)
    tok = np.arange(LAT)
    ang = np.concatenate([(tok // GRID_W).astype(np.float32)[:, None] * inv,
                          (tok % GRID_W).astype(np.float32)[:, None] * inv], axis=-1)
    feat = (i % HALF) // 2
    blocks["cos"] = np.cos(ang).T[feat]
    blocks["sin"] = np.sin(ang).T[feat]
    return {k: np.asarray(v, np.float32) for k, v in blocks.items()}


def constant_places():
    at, places = 0, {}
    for k, v in constant_blocks().items():
        places[k] = (at, v.shape[1])
        at += v.shape[1]
    return places, at


class Steps:

    def __init__(self, eng, sem):
        self.eng, self.sem, self.n, self.i, self.stride = eng, sem, 0, None, 0

    def did(self, ins):
        ins.then_inc(self.sem, 1)
        self.n += 1
        return self.n + self.i * self.stride if self.i is not None else self.n

    def link(self, ins):
        self.eng.wait_ge(self.sem, self.did(ins))

    @contextmanager
    def loop(self, count, stride):
        with self.eng.Fori(0, count) as i:
            before = self.n
            self.i, self.stride = i, stride
            yield i
            assert self.n - before == stride, (self.n - before, stride)
        self.i, self.n = None, before + count * stride


SEMAPHORES = """
 consts_landed rows_landed x_landed lam_landed unit_started mod_started
 rows_turned params_ready x_turned x_updated cond_ready banks_set pads_zeroed
 m_rows_done m_rows_copied m_turned m_ready
 acc_done acc_freed silu_done scales_ready
 out_squared post_sum post_root
 x_squared square_summed pre_root h_ready
 act_steps dve_steps
 conv_done
 ab_turned b_sigmoid a_abs a_exp g_ready G_summed G_exp head_closed
 qk_squared v_fixed pack_fixed qk_sums qk_roots qk_normed kv_turned grams decays_spread
 kv_copied exps_done tail_done qdec_done kdec_done diffs_done decays_done masked_done m2_done
 t_turned t_copied p1_done p1_masked ty_done ty_updated
 ks_done r_done v_done v_scaled o_done o_added s_done s_updated
 o_squared o_sum o_root
 lam_exp
 qk_fixed turned_back rotated scores_done max_done probs_done mixed_done a_turned a_copied
 attn_done attn_squared attn_sum attn_root
 y_turned y_copied out_landed
""".split()



def hybrid_backbone(nc, x, c, ctx_in, c_ctx, w_mod, b_mod, norm_pre, norm_post, ffn_w_in, ffn_w_out,
                    gdn_w_in, gdn_conv, gdn_A_log, gdn_dt_bias, gdn_o_gain, gdn_w_out,
                    diff_w_in, diff_lambda, diff_subln, diff_w_out, consts, out):
    places, n_const = constant_places()
    unit0, group0, mod0 = [], [], {}
    u = g = 0
    m = MOD_FIRST
    for n, (kind, _, _) in enumerate(SUBS):
        unit0.append(u)
        group0.append(g)
        u += UNITS[kind]
        g += GROUPS[kind]
        if n in MOD_INSIDE:
            mod0[n] = m
            m += MOD_INSIDE[n]
    assert m == MVEC * KC
    ffns = [n for n, s in enumerate(SUBS) if s[0] == "ffn"]

    with ExitStack() as ctx:
        def sb(name, shape):
            return ctx.enter_context(nc.sbuf_tensor(name, shape, F32))

        S = {name: ctx.enter_context(nc.semaphore(name)) for name in SEMAPHORES}
        w_landed = [ctx.enter_context(nc.semaphore(f"w_landed{i}")) for i in range(SLOTS)]
        m_landed = [ctx.enter_context(nc.semaphore(f"m_landed{i}")) for i in range(MSLOTS)]

        bank = ctx.enter_context(nc.psum_tensor("bank", [P, 8, 512], F32))

        cst = sb("cst", [P, n_const])
        xs = sb("xs", [P, KC, TOK])
        hs = sb("hs", [P, KC, TOK])
        big = sb("big", [P, 4 * KC, TOK])
        ring = sb("ring", [P, SLOTS, UNIT])
        mring = sb("mring", [P, MSLOTS, D])
        prm = sb("prm", [P, len(ROWS), P])
        cond = sb("cond", [P, KC, 2])
        mrow = sb("mrow", [P, 256])
        modv = sb("modv", [P, MVEC, 2, KC])
        pre_scale = sb("pre_scale", [P, len(SUBS), 2, KC])
        post_scale = sb("post_scale", [P, len(SUBS), 2, KC])
        root = sb("root", [P, TOK])
        lamv = sb("lamv", [P, 8])
        pack_w = 5 * 2 * NC
        pack = sb("pack", [P, HEADS, pack_w])
        lam_row = sb("lam_row", [P, 4 * HALF])
        alog = sb("alog", [P, 2 * HEADS])
        dtb = sb("dtb", [P, 2 * HEADS])
        eps_col = sb("eps_col", [P, 4])
        ROOM = 7464
        room = sb("room", [P, ROOM])

        class Carver:

            def __init__(self, area, size):
                self.area, self.size, self.at = area, size, 0

            def __call__(self, *shape):
                ap = self.area[:, self.at:self.at + int(np.prod(shape))]
                self.at += int(np.prod(shape))
                assert self.at <= self.size, (self.at, self.size)
                if len(shape) == 2:
                    ap = ap.rearrange("p (a b) -> p a b", a=shape[0])
                return ap

        def k_(name):
            at, n = places[name]
            return cst[:, at:at + n]

        ident, ones = k_("ident"), k_("ones")
        flat_big = big[:, :, :].rearrange("p a b -> p (a b)")
        flat_hs = hs[:, :, :].rearrange("p a b -> p (a b)")

        carve = Carver(room, ROOM)
        sg = carve(2, TOK)
        sq = carve(2, TOK)
        ssq = carve(TOK)
        carve = Carver(room, ROOM)
        convp = carve(2, 2 * (LAT + 2 * PAD))
        conv_in = convp.rearrange("p a (s t) -> p a s t", s=2)
        convs = carve(2, TOK)
        ab = carve(TOK)
        gate_t = carve(7, NC * 2 * HEADS)
        carve = Carver(room, ROOM)
        qk_n = carve(2, TOK)
        vfix = carve(TOK)
        vtok = carve(TOK)
        ktok = carve(TOK)
        ktail = carve(2, TOK)
        kdec = carve(2, TOK)
        qdec = carve(2, TOK)
        intra = carve(2, TOK)
        state = carve(2, P)
        r0 = carve(2, P)
        vnew = carve(2, P)
        hpack = carve(pack_w)
        osum = vfix
        orin = ktok
        carve = Carver(flat_hs, KC * TOK)
        expg = carve(2, TOK)
        m2t = carve(2, TOK)
        yy = carve(2, TOK)
        p1m = carve(2, TOK)
        tt_ = expg
        gt = yy
        carve = Carver(room, ROOM)
        qraw = carve(2, LAT)
        kall = carve(TOK)
        qrot = carve(LAT)
        rtmp = carve(2, LAT)
        rtmp2 = carve(2, LAT)
        vhead = carve(NC, P)
        amix = carve(2, TOK)
        at_ = carve(NC, LAT)
        stat = carve(24)
        oat = carve(LAT)
        rat = carve(LAT)
        lam_prod = amix[:, 0, 0:2 * HALF].rearrange("p (a b) -> p a b", a=2)
        carve = Carver(flat_hs, KC * TOK)
        probs = carve(4, TOK)
        v_rows = flat_big[:, 2 * KC * TOK:3 * KC * TOK].rearrange("p (t d) -> p t d", t=NC)

        def chunks(a):
            return a.rearrange("p (n e) -> p n e", n=NC)

        def per_token(f, d):
            return hpack[:, (f * 2 + d) * NC:(f * 2 + d + 1) * NC].unsqueeze(2).to_broadcast([P, NC, P])

        def col(f, d, t):
            return hpack[:, (f * 2 + d) * NC + t:(f * 2 + d) * NC + t + 1]

        rows_in = flat_big[:, 0:len(ROWS) * P].rearrange("p (a b) -> p a b", a=len(ROWS))
        x_in = flat_big[:, 1024:1024 + NC * D].rearrange("p (t d) -> p t d", t=NC)
        y_out = flat_big[:, 0:2 * D].rearrange("p (t d) -> p t d", t=2)
        names = list(ROWS)
        b_mod_col = [prm[:, names.index(f"b_mod{l}"), :] for l in range(DEPTH)]
        norms_col = prm[:, names.index("norms"), :]
        conv_col = prm[:, names.index("conv"), :]
        cond_col = prm[:, names.index("cond"), :]

        def lo(n):
            return CTX if n >= 4 else 0

        def pre_lo(n):
            return CTX if n > 4 else 0

        def seg(first):
            both = [(slice(0, CTX), 1), (slice(CTX, TOK), 0)]
            return both[1:] if first else both

        block = ctx.enter_context(nc.Block())

        def slot(s, k, width):
            return ring[:, s % SLOTS, 0:k * width].rearrange("p (k n) -> p k n", k=k)

        @block.sync
        def _(sp):
            sp.dma_start(cst[:, :], consts).then_inc(S["consts_landed"], 16)
            small = [
                (rows_in[0:48, 0, :], norm_pre.rearrange("l s (c p) -> (l s c) p", p=P)),
                (rows_in[48:96, 0, :], norm_post.rearrange("l s (c p) -> (l s c) p", p=P)),
                (rows_in[0:120, 1, :], gdn_conv.rearrange("o t (c p) -> (o t c) p", p=P)),
                (rows_in[0:72, 2, :], b_mod[0].rearrange("(c p) -> c p", p=P)),
                (rows_in[0:72, 3, :], b_mod[1].rearrange("(c p) -> c p", p=P)),
                (rows_in[0:8, 4, :], c.rearrange("o (c p) -> (o c) p", p=P)),
                (rows_in[8:16, 4, :], c_ctx.rearrange("(c p) -> c p", p=P)),
                (rows_in[16:17, 4, :], gdn_o_gain),
                (rows_in[17:18, 4, :], diff_subln),
            ]
            assert len(small) == N_SMALL
            for dst, src in small:
                sp.dma_start(dst, src).then_inc(S["rows_landed"], 16)
            sp.dma_start(x_in[:, 0:2, :], ctx_in[0].rearrange("(t p) d -> p t d", p=P)).then_inc(S["x_landed"], 16)
            sp.dma_start(x_in[:, 2:4, :], x[0].rearrange("(t p) d -> p t d", p=P)).then_inc(S["x_landed"], 16)
            for dst, src in ((alog[:, :], gdn_A_log), (dtb[:, :], gdn_dt_bias)):
                sp.dma_start(dst, src.rearrange("o d h -> o (d h)").to_broadcast([P, 2 * HEADS])
                             ).then_inc(S["lam_landed"], 16)
            sp.dma_start(lam_row[:, :], diff_lambda.rearrange("o a b -> o (a b)").to_broadcast([P, 4 * HALF])
                         ).then_inc(S["lam_landed"], 16)

            def load(w, unit, s, k, width, at, rows=P):
                sp.wait_ge(S["unit_started"], unit + 1)
                sp.dma_start(slot(s, k, width), w[:, ds(at, width)].rearrange("(k p) n -> p k n", p=rows)
                             ).then_inc(w_landed[s % SLOTS], 16)

            for n, (kind, l, j) in enumerate(SUBS):
                u = unit0[n]
                if kind == "ffn":
                    w_in, w_out = ffn_w_in[l, j // 2], ffn_w_out[l, j // 2]
                    with sp.Fori(0, FC // 4) as it:
                        for r in range(4):
                            load(w_in, u + it * 4 + r, u + r, KC, 256, it * 512 + (r // 2) * 256 + (r % 2) * DFF)
                    last = FC // 4 * 4
                    for r in range(2):
                        load(w_in, u + last + r, u + last + r, KC, 256, (FC - 2) * P + r * DFF)
                    uo = u + FC
                    with sp.Fori(0, KC // 4) as it:
                        for r in range(4):
                            load(w_out, uo + it * 4 + r, uo + r, FC, P, it * 512 + r * P)
                else:
                    w_in, w_out = (gdn_w_in[0], gdn_w_out[0]) if kind == "gdn" else (diff_w_in[0], diff_w_out[0])
                    trips = 4 if kind == "gdn" else 3
                    with sp.Fori(0, trips) as it:
                        for r in range(4):
                            load(w_in, u + it * 4 + r, u + r, KC, 256, it * 1024 + r * 256)
                    uo = u + 4 * trips
                    if kind == "gdn":
                        load(w_in, uo, uo, KC, 4 * HEADS, 4 * D)
                        uo += 1
                    for r in range(4):
                        load(w_out, uo + r, uo + r, KC, 256, r * 256)

            sp.wait_ge(S["y_copied"], KC)
            sp.dma_start(out[0].rearrange("(t p) d -> p t d", p=P), y_out).then_inc(S["out_landed"], 16)
            sp.wait_ge(S["out_landed"], 16)

        @block.gpsimd
        def _(pool):
            def mod_loads(l):
                with pool.Fori(0, 9) as v:
                    for k in range(KC):
                        pool.wait_ge(S["mod_started"], l * 9 * KC + v * KC + k + 1)
                        pool.dma_start(mring[:, k % MSLOTS, :], w_mod[l, k * P:(k + 1) * P, ds(v * D, D)]
                                       ).then_inc(m_landed[k % MSLOTS], 16)

            mod_loads(0)

            with pool.Fori(0, HEADS) as h:
                pool.wait_ge(S["head_closed"], h + 1)
                nc.gpsimd.tensor_copy(vfix, big[:, ds(h + 2 * KC, 1), :]).then_inc(S["v_fixed"], 1)
                nc.gpsimd.tensor_copy(hpack, pack[:, ds(h, 1), :]).then_inc(S["pack_fixed"], 1)
                pool.wait_ge(S["pack_fixed"], h + 1)
                pool.wait_ge(S["kv_copied"], h * 2 + 1)
                for d in range(2):
                    nc.gpsimd.tensor_tensor(chunks(ktail[:, d, :]), chunks(ktok), per_token(4, d),
                                            ALU.mult).then_inc(S["tail_done"], 1)
                for d in range(2):
                    pool.wait_ge(S["exps_done"], h * 2 + d + 1)
                    nc.gpsimd.tensor_tensor(qdec[:, d, :], qk_n[:, 1, :], expg[:, d, :],
                                            ALU.mult).then_inc(S["qdec_done"], 1)
            mod_loads(1)

            with pool.Fori(0, HEADS) as h:
                pool.wait_ge(S["head_closed"], h + (HEADS + 2))
                nc.gpsimd.tensor_copy(qraw[:, 0, :], big[:, ds(h, 1), 0:LAT]).then_inc(S["qk_fixed"], 1)
                nc.gpsimd.tensor_copy(qraw[:, 1, :], big[:, ds(h + KC, 1), CTX:TOK]).then_inc(S["qk_fixed"], 1)
                nc.gpsimd.tensor_copy(kall[:, 0:CTX], big[:, ds(h + KC, 1), 0:CTX]).then_inc(S["qk_fixed"], 1)
                nc.gpsimd.tensor_copy(vhead, v_rows[:, :, ds(h * P, P)]).then_inc(S["v_fixed"], 1)

        @block.tensor
        def _(pe):
            mm = nc.tensor.matmul
            turn = nc.tensor.transpose

            pe.wait_ge(S["consts_landed"], 16)
            pe.wait_ge(S["rows_landed"], N_SMALL * 16)
            for b, rows in enumerate(ROWS.values()):
                turn(bank[:, b, 0:rows], rows_in[0:rows, b, :], ident[0:rows, 0:rows]).then_inc(S["rows_turned"], 1)
            pe.wait_ge(S["x_landed"], 32)
            for k in range(KC):
                b = (5 + k) % 8
                if k >= 3:
                    pe.wait_ge(S["params_ready"], k - 2)
                for t in range(NC):
                    last = turn(bank[:, b, t * P:(t + 1) * P], x_in[:, t, k * P:(k + 1) * P], ident)
                last.then_inc(S["x_turned"], 1)

            def mod_unit(i, k):
                pe.wait_ge(m_landed[k % MSLOTS], i * (KC * 16 // MSLOTS) + (k // MSLOTS + 1) * 16)
                if k == 0:
                    pe.wait_ge(S["m_rows_copied"], i + 1)
                for q in range(4):
                    last = mm(bank[32 * q:32 * q + 2, 4, 0:256], cond[:, k, :],
                              mring[:, k % MSLOTS, q * 256:(q + 1) * 256], start=(k == 0), stop=(k == KC - 1))
                    if q == 0:
                        last.then_inc(S["mod_started"], 1)
                if k == KC - 1:
                    last.then_inc(S["m_rows_done"], 1)

            def mod_turn(i):
                pe.wait_ge(S["m_rows_copied"], i + 2)
                turn(bank[:, 5, 0:P], mrow[:, 0:P], ident)
                turn(bank[:, 5, P:2 * P], mrow[:, P:2 * P], ident).then_inc(S["m_turned"], 1)

            def unit_wait(unit, s):
                s %= SLOTS
                pe.wait_ge(w_landed[s], (unit - s) * (16 // SLOTS) + 16)

            def group(g, r, w, rhs, cols=TOK, rows=P, starts=False, ready=None):
                pe.wait_ge(S["acc_freed"], g + 1)
                n_k = w.shape[1]
                for k in range(n_k):
                    if ready is not None:
                        ready(k)
                    last = mm(bank[0:rows, r % 4, 0:cols], w[:, k, :], rhs(k), start=(k == 0), stop=(k == n_k - 1))
                    if k == 0 and starts:
                        last.then_inc(S["unit_started"], 1)
                last.then_inc(S["acc_done"], 1)

            pe.wait_ge(S["cond_ready"], 1)
            pe.wait_ge(S["x_updated"], KC)
            with pe.Fori(0, MOD_FIRST // KC) as i:
                for k in range(KC):
                    mod_unit(i, k)
                mod_turn(i)

            for n, (kind, l, j) in enumerate(SUBS):
                u0, g0, c0, p0 = unit0[n], group0[n], lo(n), pre_lo(n)
                for k in range(KC):
                    pe.wait_ge(S["x_squared"], n * KC + k + 1)
                    mm(bank[:, 7, p0:TOK], ones, sq[:, k % 2, p0:TOK], start=(k == 0), stop=(k == KC - 1)
                       ).then_inc(S["square_summed"], 1)

                def h_wait(k, n=n):
                    pe.wait_ge(S["h_ready"], n * KC + k + 1)

                if kind == "ffn":
                    def pair(i, a, fresh=False):
                        for v in range(2):
                            s = u0 + a + v
                            unit_wait(u0 + i * 2 + v, s)
                            for jj in range(2):
                                pe.wait_ge(S["acc_freed"], g0 + i * 4 + (4 if jj else 2))
                                w = slot(s, KC, 256)
                                for k in range(KC):
                                    if fresh and v == 0 and jj == 0:
                                        h_wait(k)
                                    last = mm(bank[:, (g0 + 2 * v + jj) % 4, 0:TOK - c0], w[:, k, jj * P:(jj + 1) * P],
                                              hs[:, k, c0:TOK], start=(k == 0), stop=(k == KC - 1))
                                    if k == 0 and jj == 0:
                                        last.then_inc(S["unit_started"], 1)
                                last.then_inc(S["acc_done"], 1)

                    with pe.Fori(0, FC // 4) as it:
                        pair(it * 2, 0, fresh=True)
                        pair(it * 2 + 1, 2)
                    pair(FC // 2 - 1, FC // 4 * 4)

                    uo, go = u0 + FC, g0 + 2 * FC

                    def hidden_wait(k):
                        if k == 0:
                            pe.wait_ge(S["acc_freed"], go)
                        elif k >= FC - 2:
                            pe.wait_ge(S["acc_freed"], go + 2 * (k - (FC - 2)) + 2)

                    def out_four(it, with_mod):
                        for r in range(4):
                            if with_mod:
                                for m in range(6 * r, 6 * r + 6):
                                    mod_unit(it * 3 + (mod0[n] // KC + m // KC), m % KC)
                            unit_wait(uo + it * 4 + r, uo + r)
                            group(go + it * 4 + r, go + r, slot(uo + r, FC, P), lambda k: big[:, k, 0:TOK - c0],
                                  cols=TOK - c0, starts=True, ready=hidden_wait)
                            if with_mod and r > 0:
                                mod_turn(it * 3 + (mod0[n] // KC + r - 1))

                    n_mod = MOD_INSIDE.get(n, 0) // 24
                    if n_mod:
                        with pe.Fori(0, n_mod) as it:
                            out_four(it, True)
                    if n_mod < 2:
                        with pe.Fori(n_mod, 2) as it:
                            out_four(it, False)

                if kind == "gdn":
                    with pe.Fori(0, 4) as it:
                        for r in range(4):
                            unit_wait(u0 + it * 4 + r, u0 + r)
                            for jj in range(2):
                                q = 2 * r + jj
                                group(g0 + it * 8 + q, g0 + q, slot(u0 + r, KC, 256)[:, :, jj * P:(jj + 1) * P],
                                      lambda k: hs[:, k, :], starts=(jj == 0), ready=h_wait if q == 0 else None)
                    ua, ga = u0 + 16, g0 + 32
                    unit_wait(ua, ua)
                    group(ga, ga, slot(ua, KC, 4 * HEADS), lambda k: hs[:, k, :], rows=4 * HEADS, starts=True)
                    pe.wait_ge(S["acc_freed"], ga + 1 + 4)
                    for t in range(NC):
                        last = turn(bank[:, 4, t * 32:(t + 1) * 32], ab[0:32, t * P:(t + 1) * P], ident[0:32, 0:32])
                    last.then_inc(S["ab_turned"], 1)
                    pe.wait_ge(S["g_ready"], 1)
                    for d in range(2):
                        mm(bank[:, 5, d * 32:(d + 1) * 32].rearrange("p (n h) -> p n h", n=NC), k_(f"incl{d}"),
                           gate_t[:, 2, :].rearrange("p (n h) -> p n h", n=NC)[:, :, d * HEADS:(d + 1) * HEADS],
                           start=True, stop=True)
                    mm(bank[:, 6, 0:64], ones, gate_t[:, 2, :], start=True, stop=True).then_inc(S["G_summed"], 1)

                    with pe.Fori(0, HEADS) as h:
                        def each(sem, per, k):
                            pe.wait_ge(S[sem], h * per + k)

                        each("head_closed", 1, 1)
                        each("qk_squared", 2, 2)
                        mm(bank[:, 0, :], ones, p1m[:, 0, :], start=True, stop=True)
                        mm(bank[:, 1, :], ones, p1m[:, 1, :], start=True, stop=True).then_inc(S["qk_sums"], 1)
                        each("pack_fixed", 1, 1)
                        for d in range(2):
                            for t in range(NC):
                                last = mm(bank[:, 6 + d, t * P:(t + 1) * P],
                                          hpack[:, d * NC + t:d * NC + t + 1].to_broadcast([P, P]), k_(f"incl{d}"),
                                          start=True, stop=True)
                            last.then_inc(S["decays_spread"], 1)
                        each("v_fixed", 1, 1)
                        for t in range(NC):
                            turn(bank[:, 3, t * P:(t + 1) * P], vfix[:, t * P:(t + 1) * P], ident)
                        each("qk_normed", 2, 2)
                        for t in range(NC):
                            last = turn(bank[:, 2, t * P:(t + 1) * P], qk_n[:, 0, t * P:(t + 1) * P], ident)
                        last.then_inc(S["kv_turned"], 1)
                        for t in range(NC):
                            last = mm(bank[:, 4 + t // 2, (t % 2) * 256:(t % 2) * 256 + 256].rearrange("p (a b) -> p a b", a=2),
                                      qk_n[:, 0, t * P:(t + 1) * P], qk_n[:, :, t * P:(t + 1) * P], start=True, stop=True)
                        last.then_inc(S["grams"], 1)
                        for d in range(2):
                            each("m2_done", 2, d + 1)
                            if d == 0:
                                each("kv_copied", 2, 2)
                            for t in range(NC):
                                last = turn(bank[:, 2 + d, t * P:(t + 1) * P], yy[:, d, t * P:(t + 1) * P], ident)
                            last.then_inc(S["t_turned"], 1)
                        for q, w in enumerate(LEVELS):
                            for d in range(2):
                                if q == 0:
                                    each("t_copied", 2, d + 1)
                                else:
                                    each("ty_updated", 2 * len(LEVELS), 2 * (q - 1) + d + 1)
                                for t in range(NC):
                                    tc = slice(t * P, (t + 1) * P)
                                    last = mm(bank[:, d, tc], m2t[:, d, tc], tt_[:, d, tc], start=True, stop=True)
                                last.then_inc(S["p1_done"], 1)
                            for d in range(2):
                                each("p1_masked", 2 * len(LEVELS), 2 * q + d + 1)
                                for t in range(NC):
                                    tc = slice(t * P, (t + 1) * P)
                                    if w != LEVELS[-1]:
                                        mm(bank[:, 2 + d, tc], yy[:, d, tc], p1m[:, d, tc], start=True, stop=True)
                                for t in range(NC):
                                    tc = slice(t * P, (t + 1) * P)
                                    last = mm(bank[:, 4 + d, tc], p1m[:, d, tc], yy[:, d, tc], start=True, stop=True)
                                last.then_inc(S["ty_done"], 1)
                        each("kdec_done", 2, 2)
                        each("qdec_done", 2, 2)
                        each("tail_done", 2, 2)
                        for st in range(NC):
                            for d in range(2):
                                tc = slice(WALK[d][st] * P, (WALK[d][st] + 1) * P)
                                if st:
                                    each("s_updated", 6, 2 * (st - 1) + d + 1)
                                    mm(bank[:, d, 0:P], kdec[:, d, tc], state[:, d, :], start=True, stop=True
                                       ).then_inc(S["ks_done"], 1)
                            for d in range(2):
                                tc = slice(WALK[d][st] * P, (WALK[d][st] + 1) * P)
                                if st:
                                    each("r_done", 6, 2 * (st - 1) + d + 1)
                                else:
                                    each("ty_updated", 2 * len(LEVELS), 2 * (len(LEVELS) - 1) + d + 1)
                                mm(bank[:, 2 + d, 0:P], yy[:, d, tc], r0[:, d, :] if st else vtok[:, tc],
                                   start=True, stop=True).then_inc(S["v_done"], 1)
                            for d in range(2):
                                tc = slice(WALK[d][st] * P, (WALK[d][st] + 1) * P)
                                if st:
                                    each("o_added", 8, 2 * (st - 1) + d + 1)
                                    mm(bank[:, 4 + d, 0:P], state[:, d, :], qdec[:, d, tc], start=True, stop=False)
                                each("v_scaled", 8, 2 * st + d + 1)
                                if st < NC - 1:
                                    mm(bank[:, 6 + d, 0:P], ktail[:, d, tc], vnew[:, d, :], start=True, stop=True
                                       ).then_inc(S["s_done"], 1)
                                mm(bank[:, 4 + d, 0:P], vnew[:, d, :], intra[:, d, tc], start=(st == 0), stop=True
                                   ).then_inc(S["o_done"], 1)
                        each("o_squared", 1, 1)
                        mm(bank[:, 0, :], ones, orin, start=True, stop=True).then_inc(S["o_sum"], 1)

                    pe.wait_ge(S["head_closed"], HEADS + 1)
                    uo, go = u0 + 17, g0 + 33
                    for r in range(4):
                        unit_wait(uo + r, uo + r)
                        for jj in range(2):
                            q = 2 * r + jj
                            group(go + q, go + q, slot(uo + r, KC, 256)[:, :, jj * P:(jj + 1) * P],
                                  lambda k: big[:, 2 * KC + k, :], starts=(jj == 0))

                if kind == "diff":
                    for part in range(2):
                        for r in range(4):
                            ux = u0 + part * 4 + r
                            unit_wait(ux, ux)
                            for jj in range(2):
                                g = g0 + part * 8 + 2 * r + jj
                                rhs = (lambda k: hs[:, k, CTX:TOK]) if part == 0 else (lambda k: hs[:, k, :])
                                group(g, g, slot(ux, KC, 256)[:, :, jj * P:(jj + 1) * P], rhs,
                                      cols=LAT if part == 0 else TOK, starts=(jj == 0), ready=h_wait if g == g0 else None)
                    for r in range(4):
                        ux = u0 + 8 + r
                        unit_wait(ux, ux)
                        for t in range(NC):
                            g = g0 + 16 + 4 * r + t
                            pe.wait_ge(S["acc_freed"], g + 1)
                            for k in range(KC):
                                last = mm(bank[:, g % 4, 0:256], hs[:, k, t * P:(t + 1) * P], slot(ux, KC, 256)[:, k, :],
                                          start=(k == 0), stop=(k == KC - 1))
                                if k == 0 and t == 0:
                                    last.then_inc(S["unit_started"], 1)
                            last.then_inc(S["acc_done"], 1)

                    with pe.Fori(0, HEADS) as h:
                        def each(sem, per, k):
                            pe.wait_ge(S[sem], h * per + k)

                        pe.wait_ge(S["head_closed"], h + (HEADS + 2))
                        each("qk_fixed", 3, 3)
                        mm(bank[:, 0, :], k_("rot"), qraw.rearrange("p a b -> p (a b)"), start=True, stop=True
                           ).then_inc(S["turned_back"], 1)
                        each("rotated", 2, 2)
                        for t in range(2):
                            for m in range(2):
                                rows = slice(m * HALF, (m + 1) * HALF)
                                mm(bank[:, 4 + 2 * t + m, :], qrot[rows, t * P:(t + 1) * P], kall[rows, :],
                                   start=True, stop=True).then_inc(S["scores_done"], 1)
                        for t in range(2):
                            each("mixed_done", 2, t + 1)
                            for kt in range(NC):
                                last = turn(bank[:, 2 + t, kt * P:(kt + 1) * P], amix[:, t, kt * P:(kt + 1) * P], ident)
                            last.then_inc(S["a_turned"], 1)
                        each("a_copied", 2, 2)
                        pe.wait_ge(S["v_fixed"], h + (HEADS + 1))
                        for kt in range(NC):
                            last = mm(bank[:, 1, 0:LAT], vhead[:, kt, :], at_[:, kt, :], start=(kt == 0), stop=(kt == NC - 1))
                        last.then_inc(S["attn_done"], 1)
                        each("attn_squared", 1, 1)
                        mm(bank[:, 0, 0:LAT], ones, rat, start=True, stop=True).then_inc(S["attn_sum"], 1)

                    pe.wait_ge(S["head_closed"], 2 * HEADS + 2)
                    uo, go = u0 + 12, g0 + 32
                    for r in range(4):
                        unit_wait(uo + r, uo + r)
                        for jj in range(2):
                            q = 2 * r + jj
                            group(go + q, go + q, slot(uo + r, KC, 256)[:, :, jj * P:(jj + 1) * P],
                                  lambda k: big[:, 3 * KC + k, 0:LAT], cols=LAT, starts=(jj == 0))

                pe.wait_ge(S["acc_freed"], group0[n] + GROUPS[kind] + 4)
                mm(bank[:, 6, c0:TOK], ones, ssq[:, c0:TOK], start=True, stop=True).then_inc(S["post_sum"], 1)

            for k in range(KC):
                pe.wait_ge(S["x_updated"], len(SUBS) * KC + k + 1)
                if k >= 4:
                    pe.wait_ge(S["y_copied"], k - 3)
                for t in range(2):
                    last = turn(bank[:, k % 4, t * P:(t + 1) * P], xs[:, k, CTX + t * P:CTX + (t + 1) * P], ident)
                last.then_inc(S["y_turned"], 1)

        @block.scalar
        def _(act):
            fn = nc.scalar.activation
            steps = Steps(act, S["act_steps"])

            act.wait_ge(S["params_ready"], len(ROWS))
            fn(cond[:, :, :].rearrange("p k v -> p v k"),
               cond_col[:, 0:16].rearrange("p (v k) -> p v k", v=2), ACT.Silu).then_inc(S["cond_ready"], 1)

            for n, (kind, l, j) in enumerate(SUBS):
                g0, c0, p0 = group0[n], lo(n), pre_lo(n)
                width = TOK - c0
                for k in range(KC):
                    act.wait_ge(S["x_updated"], n * KC + k + 1)
                    if k >= 2:
                        act.wait_ge(S["square_summed"], n * KC + k - 1)
                    fn(sq[:, k % 2, p0:TOK], xs[:, k, p0:TOK], ACT.Square).then_inc(S["x_squared"], 1)
                act.wait_ge(S["square_summed"], (n + 1) * KC)
                fn(root[:, p0:TOK], bank[:, 7, p0:TOK], ACT.Sqrt, bias=eps_col[:, 0:1], scale=1.0 / D).then_inc(S["pre_root"], 1)

                if kind == "ffn":
                    jj0 = ffns.index(n) * FC

                    def gates(i, r):
                        for jj in range(2):
                            act.wait_ge(S["acc_done"], g0 + i * 4 + jj + 1)
                            act.wait_ge(S["acc_freed"], g0 + i * 4 + 2 * jj + 2)
                            fn(sg[:, jj, 0:width], bank[:, (g0 + jj) % 4, 0:width], ACT.Silu).then_inc(S["silu_done"], 1)

                    with act.Fori(0, FC // 2) as i:
                        gates(i, 0)
                    go = g0 + 2 * FC

                if kind == "gdn":
                    def conv_chunk(i, q):
                        g = g0 + i * 8 + q
                        act.wait_ge(S["acc_done"], g + 1)
                        fn(conv_in[:, q % 2, :, PAD:PAD + LAT], bank[:, (g0 + q) % 4, :].rearrange("p (s t) -> p s t", s=2),
                           ACT.Copy).then_inc(S["acc_freed"], 1)
                        act.wait_ge(S["conv_done"], i * 8 + q + 1)
                        steps.did(fn(big[:, ds(i * 8 + q, 1), :], convs[:, q % 2, :], ACT.Silu))

                    act.wait_ge(S["pads_zeroed"], 1)
                    with steps.loop(3, KC) as i:
                        for q in range(KC):
                            conv_chunk(i, q)
                    for q in range(KC):
                        g = g0 + 24 + q
                        act.wait_ge(S["acc_done"], g + 1)
                        fn(big[:, 3 * KC + q, :], bank[:, g % 4, :], ACT.Silu).then_inc(S["acc_freed"], 1)
                    g = g0 + 32
                    act.wait_ge(S["acc_done"], g + 1)
                    fn(ab[0:32, :], bank[0:32, g % 4, :], ACT.Copy).then_inc(S["acc_freed"], 1)
                    act.wait_ge(S["ab_turned"], 1)
                    act.wait_ge(S["a_abs"], 1)
                    fn(gate_t[:, 3, :].rearrange("p (n h) -> p n h", n=NC),
                       bank[:, 4, 0:P].rearrange("p (n h) -> p n h", n=NC)[:, :, 16:32], ACT.Sigmoid).then_inc(S["b_sigmoid"], 1)
                    steps.link(fn(gate_t[:, 1, :], gate_t[:, 1, :], ACT.Exp, scale=-1.0))
                    fn(gate_t[:, 1, :], gate_t[:, 1, :], ACT.Ln, bias=eps_col[:, 2:3])
                    fn(alog[:, :], alog[:, :], ACT.Exp).then_inc(S["a_exp"], 1)
                    act.wait_ge(S["G_exp"], 1)
                    fn(gate_t[:, 4, :], bank[:, 6, 0:64], ACT.Exp)
                    fn(gate_t[:, 5, :], gate_t[:, 5, :], ACT.Exp).then_inc(S["G_exp"], 1)

                    with act.Fori(0, HEADS) as h:
                        def each(sem, per, k):
                            act.wait_ge(S[sem], h * per + k)

                        each("head_closed", 1, 1)
                        fn(p1m[:, 0, :], big[:, ds(h, 1), :], ACT.Square).then_inc(S["qk_squared"], 1)
                        fn(p1m[:, 1, :], big[:, ds(h + KC, 1), :], ACT.Square).then_inc(S["qk_squared"], 1)
                        each("qk_sums", 1, 1)
                        fn(intra[:, 0, :], bank[:, 0, :], ACT.Sqrt, bias=eps_col[:, 1:2], scale=float(P)).then_inc(S["qk_roots"], 1)
                        fn(intra[:, 1, :], bank[:, 1, :], ACT.Sqrt, bias=eps_col[:, 0:1], scale=1.0).then_inc(S["qk_roots"], 1)
                        for d in range(2):
                            each("decays_spread", 2, d + 1)
                            fn(expg[:, d, :], bank[:, 6 + d, :], ACT.Exp).then_inc(S["exps_done"], 1)
                        each("kv_turned", 1, 1)
                        fn(ktok, bank[:, 2, :], ACT.Copy).then_inc(S["kv_copied"], 1)
                        fn(vtok, bank[:, 3, :], ACT.Copy).then_inc(S["kv_copied"], 1)
                        for d in range(2):
                            each("diffs_done", 2, d + 1)
                            fn(gt[:, d, :], gt[:, d, :], ACT.Exp).then_inc(S["decays_done"], 1)
                        for d in range(2):
                            each("t_turned", 2, d + 1)
                            if d == 0:
                                each("kdec_done", 2, 2)
                                each("qdec_done", 2, 2)
                            fn(tt_[:, d, :], bank[:, 2 + d, :], ACT.Copy).then_inc(S["t_copied"], 1)
                        for st in range(NC):
                            for d in range(2):
                                t = WALK[d][st]
                                each("v_done", 8, 2 * st + d + 1)
                                if st:
                                    each("o_done", 8, 2 * (st - 1) + d + 1)
                                fn(vnew[:, d, :], bank[:, 2 + d, 0:P], ACT.Copy, scale=col(2, d, t)).then_inc(S["v_scaled"], 1)
                        each("o_added", 8, 8)
                        fn(orin, osum, ACT.Square).then_inc(S["o_squared"], 1)
                        each("o_sum", 1, 1)
                        fn(orin, bank[:, 0, :], ACT.Sqrt, bias=eps_col[:, 0:1], scale=1.0 / P).then_inc(S["o_root"], 1)
                    go = g0 + 33

                if kind == "diff":
                    for q in range(KC):
                        g = g0 + q
                        act.wait_ge(S["acc_done"], g + 1)
                        fn(big[:, q, 0:LAT], bank[:, g % 4, 0:LAT], ACT.Copy).then_inc(S["acc_freed"], 1)
                    for q in range(KC):
                        g = g0 + KC + q
                        act.wait_ge(S["acc_done"], g + 1)
                        fn(big[:, KC + q, :], bank[:, g % 4, :], ACT.Copy).then_inc(S["acc_freed"], 1)
                    for r in range(4):
                        for t in range(NC):
                            g = g0 + 16 + 4 * r + t
                            act.wait_ge(S["acc_done"], g + 1)
                            fn(v_rows[:, t, r * 256:(r + 1) * 256], bank[:, g % 4, 0:256], ACT.Copy).then_inc(S["acc_freed"], 1)
                    act.wait_ge(S["lam_exp"], 1)
                    fn(lamv[:, 2:4], lamv[:, 0:2], ACT.Exp).then_inc(S["lam_exp"], 1)

                    with act.Fori(0, HEADS) as h:
                        def each(sem, per, k):
                            act.wait_ge(S[sem], h * per + k)

                        for t in range(2):
                            for m in range(2):
                                k = 2 * t + m
                                each("max_done", 4, k + 1)
                                fn(probs[:, k, :], bank[:, 4 + k, :], ACT.Exp, bias=stat[:, 4 + k:5 + k], scale=HALF ** -0.5,
                                   accum_out=stat[:, 8 + k:9 + k]).then_inc(S["probs_done"], 1)
                        for t in range(2):
                            each("a_turned", 2, t + 1)
                            fn(at_[:, :, t * P:(t + 1) * P], bank[:, 2 + t, :].rearrange("p (k q) -> p k q", k=NC),
                               ACT.Copy).then_inc(S["a_copied"], 1)
                        each("attn_done", 1, 1)
                        fn(oat, bank[:, 1, 0:LAT], ACT.Copy)
                        fn(rat, bank[:, 1, 0:LAT], ACT.Square).then_inc(S["attn_squared"], 1)
                        each("attn_sum", 1, 1)
                        fn(rat, bank[:, 0, 0:LAT], ACT.Sqrt, bias=eps_col[:, 0:1], scale=1.0 / P).then_inc(S["attn_root"], 1)
                    go = g0 + 32

                with act.Fori(0, 2) as i:
                    for r in range(4):
                        act.wait_ge(S["acc_done"], go + i * 4 + r + 1)
                        act.wait_ge(S["acc_freed"], go + i * 4 + r + 3)
                        acc = bank[:, (go + r) % 4, 0:width].unsqueeze(1)
                        fn(hs[:, ds(i * 4 + r, 1), c0:TOK], acc, ACT.Copy)
                        fn(sq[:, r % 2, c0:TOK].unsqueeze(1), acc, ACT.Square).then_inc(S["out_squared"], 1)
                act.wait_ge(S["post_sum"], n + 1)
                fn(root[:, c0:TOK], bank[:, 6, c0:TOK], ACT.Sqrt, bias=eps_col[:, 0:1], scale=1.0 / D).then_inc(S["post_root"], 1)

            for k in range(KC):
                act.wait_ge(S["y_turned"], k + 1)
                fn(y_out[:, :, k * P:(k + 1) * P], bank[:, k % 4, 0:2 * P].rearrange("p (t f) -> p t f", t=2),
                   ACT.Copy).then_inc(S["y_copied"], 1)

        @block.vector
        def _(dve):
            v_ = nc.vector
            steps = Steps(dve, S["dve_steps"])

            v_.memset(eps_col[:, 0:1], EPS).then_inc(S["unit_started"], SLOTS - 1)
            v_.memset(eps_col[:, 1:2], EPS * P).then_inc(S["mod_started"], MSLOTS - 1)
            steps.did(v_.memset(eps_col[:, 2:3], 1.0))
            for b, rows in enumerate(ROWS.values()):
                dve.wait_ge(S["rows_turned"], b + 1)
                v_.tensor_copy(prm[:, b, 0:rows], bank[:, b, 0:rows]).then_inc(S["params_ready"], 1)
            for k in range(KC):
                dve.wait_ge(S["x_turned"], k + 1)
                v_.tensor_copy(xs[:, k, :], bank[:, (5 + k) % 8, :]).then_inc(S["x_updated"], 1)
            dve.wait_ge(S["x_updated"], KC)
            v_.memset(bank[:, 4, 0:256], 0.0).then_inc(S["m_rows_copied"], 1)
            v_.memset(lamv[:, 7:8], 0.0).then_inc(S["acc_freed"], 4)

            def mod_rows(i):
                dve.wait_ge(S["m_rows_done"], i + 1)
                v_.tensor_copy(mrow[:, :], bank[:, 4, 0:256]).then_inc(S["m_rows_copied"], 1)

            def mod_columns(i, l):
                dve.wait_ge(S["m_turned"], i + 1)
                turned = bank[:, 5, 0:256].rearrange("p (t q v) -> p v q t", t=2, q=4)[:, 0:2]
                bias = b_mod_col[l][:, ds((i - l * 9) * KC, KC)].rearrange("p (q t) -> p q t", t=2)
                for v in range(2):
                    last = v_.tensor_tensor(modv[:, ds(i, 1), v, :].rearrange("p o (q t) -> p (o q) t", t=2),
                                            turned[:, v], bias, ALU.add)
                last.then_inc(S["m_ready"], 1)

            with dve.Fori(0, MOD_FIRST // KC) as i:
                mod_rows(i)
                mod_columns(i, 0)

            for n, (kind, l, j) in enumerate(SUBS):
                g0, c0, p0 = group0[n], lo(n), pre_lo(n)
                width = TOK - c0
                m = l * 9 + j * 3
                dve.wait_ge(S["m_ready"], m + 3)
                at = l * 24 + j * KC
                v_.scalar_tensor_tensor(pre_scale[:, n], modv[:, m + 1], 1.0,
                                        norms_col[:, at:at + KC].unsqueeze(1).to_broadcast([P, 2, KC]), ALU.add, ALU.mult)
                steps.did(v_.scalar_tensor_tensor(
                    post_scale[:, n], modv[:, m + 2], 0.5 if kind == "ffn" else 1.0,
                    norms_col[:, 48 + at:48 + at + KC].unsqueeze(1).to_broadcast([P, 2, KC]), ALU.mult, ALU.mult))

                dve.wait_ge(S["pre_root"], n + 1)
                steps.link(v_.reciprocal(root[:, p0:TOK], root[:, p0:TOK]))
                with steps.loop(KC // 2, 2) as i:
                    for r in range(2):
                        done = steps.did(v_.tensor_tensor(hs[:, ds(i * 2 + r, 1), p0:TOK], xs[:, ds(i * 2 + r, 1), p0:TOK],
                                                          root[:, p0:TOK].unsqueeze(1), ALU.mult))
                    dve.wait_ge(steps.sem, done)
                    for r in range(2):
                        for cols, v in seg(p0):
                            last = v_.tensor_scalar(hs[:, ds(i * 2 + r, 1), cols], hs[:, ds(i * 2 + r, 1), cols],
                                                    pre_scale[:, n, v, ds(i * 2 + r, 1)], modv[:, m, v, ds(i * 2 + r, 1)],
                                                    ALU.mult, ALU.add)
                        last.then_inc(S["h_ready"], 1)

                if kind == "ffn":
                    s0 = ffns.index(n) * FC
                    with dve.Fori(0, FC // 2) as i:
                        for jj in range(2):
                            dve.wait_ge(S["acc_done"], g0 + i * 4 + jj + 3)
                            dve.wait_ge(S["silu_done"], s0 + i * 2 + jj + 1)
                            v_.tensor_tensor(big[:, ds(i * 2 + jj, 1), 0:width], bank[:, (g0 + 2 + jj) % 4, 0:width].unsqueeze(1),
                                             sg[:, jj, 0:width].unsqueeze(1), ALU.mult).then_inc(S["acc_freed"], 2)
                    go = g0 + 2 * FC

                if kind == "gdn":
                    v_.memset(convp, 0.0).then_inc(S["pads_zeroed"], 1)
                    with steps.loop(3, KC * (TAPS - 1)) as i:
                        for q in range(KC):
                            dve.wait_ge(S["acc_freed"], g0 + 4 + i * KC + q + 1)
                            o = convs[:, q % 2, :].rearrange("p (s t) -> p s t", s=2)

                            def tap(t, i=i, q=q):
                                return conv_col[:, ds(i * KC + (t * 3 * KC + q), 1)]
                            steps.link(v_.tensor_scalar(o, conv_in[:, q % 2, :, 0:LAT], tap(0), None, ALU.mult))
                            for t in range(1, TAPS):
                                last = v_.scalar_tensor_tensor(o, conv_in[:, q % 2, :, t:t + LAT], tap(t), o, ALU.mult, ALU.add)
                                if t < TAPS - 1:
                                    steps.link(last)
                            last.then_inc(S["conv_done"], 1)

                    def by_token(a):
                        return gate_t[:, a, :].rearrange("p (n h) -> p n h", n=NC)

                    def over_tokens(a):
                        return a.unsqueeze(1).to_broadcast([P, NC, 2 * HEADS])

                    dve.wait_ge(S["ab_turned"], 1)
                    dve.wait_ge(S["lam_landed"], 48)
                    steps.link(v_.tensor_tensor(by_token(0), bank[:, 4, 0:P].rearrange("p (n h) -> p n h", n=NC)[:, :, 0:16],
                                                over_tokens(dtb[:, :]), ALU.add))
                    v_.scalar_tensor_tensor(gate_t[:, 1, :], gate_t[:, 0, :], -1.0, gate_t[:, 0, :], ALU.mult, ALU.max
                                            ).then_inc(S["a_abs"], 1)
                    steps.link(v_.tensor_scalar(gate_t[:, 6, :], gate_t[:, 0, :], 0.0, None, ALU.max))
                    dve.wait_ge(S["a_exp"], 1)
                    steps.link(v_.tensor_tensor(gate_t[:, 0, :], gate_t[:, 6, :], gate_t[:, 1, :], ALU.add))
                    v_.scalar_tensor_tensor(by_token(2), by_token(0), -1.0, over_tokens(alog[:, :]), ALU.mult, ALU.mult
                                            ).then_inc(S["g_ready"], 1)
                    dve.wait_ge(S["G_summed"], 1)
                    steps.link(v_.tensor_copy(gate_t[:, 6, :].rearrange("p (n d h) -> p d n h", n=NC, d=2),
                                              bank[:, 5, 0:64].rearrange("p (d n h) -> p d n h", d=2, n=NC)))
                    v_.tensor_tensor(gate_t[:, 5, :], bank[:, 6, 0:64], gate_t[:, 6, :], ALU.subtract).then_inc(S["G_exp"], 1)
                    dve.wait_ge(S["b_sigmoid"], 1)
                    dve.wait_ge(S["G_exp"], 2)
                    for f, src in enumerate((2, 6, 3, 4, 5)):
                        for d in range(2):
                            last = v_.tensor_copy(pack[:, :, (f * 2 + d) * NC:(f * 2 + d + 1) * NC],
                                                  gate_t[:, src, :].rearrange("p (n d h) -> p d h n", n=NC, d=2)[:, d])
                    last.then_inc(S["head_closed"], 1)

                    with steps.loop(HEADS, 16) as h:
                        def each(sem, per, k):
                            dve.wait_ge(S[sem], h * per + k)

                        def over_chunks(name):
                            return k_(name).unsqueeze(1).to_broadcast([P, NC, P])

                        each("qk_roots", 2, 2)
                        steps.did(v_.reciprocal(intra[:, 0, :], intra[:, 0, :]))
                        steps.link(v_.reciprocal(intra[:, 1, :], intra[:, 1, :]))
                        v_.tensor_tensor(qk_n[:, 1, :].unsqueeze(1), big[:, ds(h, 1), :], intra[:, 0, :].unsqueeze(1), ALU.mult
                                         ).then_inc(S["qk_normed"], 1)
                        v_.tensor_tensor(qk_n[:, 0, :].unsqueeze(1), big[:, ds(h + KC, 1), :], intra[:, 1, :].unsqueeze(1), ALU.mult
                                         ).then_inc(S["qk_normed"], 1)
                        for d in range(2):
                            each("exps_done", 2, d + 1)
                            last = steps.did(v_.tensor_tensor(chunks(gt[:, d, :]), chunks(bank[:, 6 + d, :]),
                                                              per_token(1, d), ALU.subtract))
                        dve.wait_ge(steps.sem, last)
                        for d in range(2):
                            v_.tensor_scalar(gt[:, d, :], gt[:, d, :], 0.0, None, ALU.min).then_inc(S["diffs_done"], 1)
                        each("qk_normed", 2, 2)
                        for d in range(2):
                            v_.tensor_tensor(kdec[:, d, :], qk_n[:, 0, :], expg[:, d, :], ALU.mult).then_inc(S["kdec_done"], 1)
                        for d in range(2):
                            each("decays_done", 2, d + 1)
                            steps.did(v_.tensor_tensor(chunks(p1m[:, d, :]), chunks(gt[:, d, :]), over_chunks(f"strict{d}"), ALU.mult))
                            last = steps.did(v_.tensor_tensor(chunks(intra[:, d, :]), chunks(gt[:, d, :]), over_chunks(f"incl{d}"), ALU.mult))
                        dve.wait_ge(steps.sem, last)
                        for d in range(2):
                            last = steps.did(v_.tensor_tensor(chunks(p1m[:, d, :]), chunks(p1m[:, d, :]), per_token(2, d), ALU.mult))
                        each("grams", 1, 1)
                        gram = bank[:, 4:6, :].rearrange("p b f -> p (b f)").rearrange("p (t a c) -> p t a c", t=NC, a=2)
                        for d in range(2):
                            v_.tensor_tensor(chunks(intra[:, d, :]), gram[:, :, 1, :], chunks(intra[:, d, :]), ALU.mult)
                        dve.wait_ge(steps.sem, last)
                        for d in range(2):
                            last = steps.did(v_.tensor_tensor(chunks(m2t[:, d, :]), gram[:, :, 0, :], chunks(p1m[:, d, :]), ALU.mult))
                        dve.wait_ge(steps.sem, last)
                        for d in range(2):
                            last = steps.did(v_.tensor_tensor(chunks(yy[:, d, :]), chunks(m2t[:, d, :]), over_chunks(f"pair{d}"), ALU.mult))
                        dve.wait_ge(steps.sem, last)
                        for d in range(2):
                            v_.tensor_tensor(chunks(yy[:, d, :]), chunks(yy[:, d, :]), over_chunks("ident"), ALU.add
                                             ).then_inc(S["m2_done"], 1)
                        n_lev = len(LEVELS)
                        for q, w in enumerate(LEVELS):
                            for d in range(2):
                                each("p1_done", 2 * n_lev, 2 * q + d + 1)
                                v_.tensor_tensor(chunks(p1m[:, d, :]), chunks(bank[:, d, :]), over_chunks(f"lev{d}_{w}"),
                                                 ALU.mult).then_inc(S["p1_masked"], 1)
                            for d in range(2):
                                each("ty_done", 2 * n_lev, 2 * q + d + 1)
                                if w != LEVELS[-1]:
                                    v_.tensor_tensor(tt_[:, d, :], tt_[:, d, :], bank[:, 2 + d, :], ALU.subtract)
                                v_.tensor_tensor(yy[:, d, :], yy[:, d, :], bank[:, 4 + d, :], ALU.subtract
                                                 ).then_inc(S["ty_updated"], 1)
                        for st in range(NC):
                            for d in range(2):
                                if st:
                                    t = WALK[d][st]
                                    each("ks_done", 6, 2 * (st - 1) + d + 1)
                                    v_.tensor_tensor(r0[:, d, :], vtok[:, t * P:(t + 1) * P], bank[:, d, 0:P], ALU.subtract
                                                     ).then_inc(S["r_done"], 1)
                            if st < NC - 1:
                                for d in range(2):
                                    each("s_done", 6, 2 * st + d + 1)
                                    if st == 0:
                                        last = v_.tensor_copy(state[:, d, :], bank[:, 6 + d, 0:P])
                                    else:
                                        each("s_updated", 6, 2 * (st - 1) + d + 1)
                                        last = v_.scalar_tensor_tensor(state[:, d, :], state[:, d, :], col(3, d, WALK[d][st]),
                                                                       bank[:, 6 + d, 0:P], ALU.mult, ALU.add)
                                    last.then_inc(S["s_updated"], 1)
                            if st % 2:
                                each("o_added", 8, 2 * st)
                            for d in range(2):
                                t = WALK[d][st]
                                each("o_done", 8, 2 * st + d + 1)
                                o = osum[:, t * P:(t + 1) * P]
                                if st % 2:
                                    last = v_.tensor_tensor(o, o, bank[:, 4 + d, 0:P], ALU.add)
                                else:
                                    last = v_.tensor_copy(o, bank[:, 4 + d, 0:P])
                                last.then_inc(S["o_added"], 1)
                        each("o_root", 1, 1)
                        steps.link(v_.reciprocal(orin, orin))
                        steps.link(v_.tensor_tensor(osum, osum, orin, ALU.mult))
                        v_.scalar_tensor_tensor(big[:, ds(h + 2 * KC, 1), :], osum.unsqueeze(1), cond_col[:, 16:17],
                                                big[:, ds(h + 3 * KC, 1), :], ALU.mult, ALU.mult).then_inc(S["head_closed"], 1)
                    go = g0 + 33

                if kind == "diff":
                    lp = lam_row[:, :].rearrange("p (a b c) -> p a b c", a=2, b=2)
                    steps.link(v_.tensor_tensor(lam_prod[:, :, :], lp[:, :, 0, :], lp[:, :, 1, :], ALU.mult))
                    v_.tensor_reduce(lamv[:, 0:2], lam_prod[:, :, :], axis=AX_X, op=ALU.add).then_inc(S["lam_exp"], 1)
                    dve.wait_ge(S["lam_exp"], 2)
                    steps.link(v_.tensor_tensor(lamv[:, 4:5], lamv[:, 3:4], lamv[:, 2:3], ALU.subtract))
                    v_.tensor_scalar(lamv[:, 5:6], lamv[:, 4:5], -LAM_INIT, None, ALU.add)
                    v_.tensor_scalar(lamv[:, 6:7], cond_col[:, 17:18], 1.0 - LAM_INIT, None, ALU.mult
                                     ).then_inc(S["head_closed"], 1)

                    with steps.loop(HEADS, 2 + 4 + 2 * 3 + 1) as h:
                        def each(sem, per, k):
                            dve.wait_ge(S[sem], h * per + k)

                        each("qk_fixed", 3, 3)
                        steps.did(v_.tensor_tensor(rtmp, qraw, k_("cos").unsqueeze(1).to_broadcast([P, 2, LAT]), ALU.mult))
                        each("turned_back", 1, 1)
                        steps.link(v_.tensor_tensor(rtmp2, bank[:, 0, :].rearrange("p (a b) -> p a b", a=2),
                                                    k_("sin").unsqueeze(1).to_broadcast([P, 2, LAT]), ALU.mult))
                        v_.tensor_tensor(qrot, rtmp[:, 0, :], rtmp2[:, 0, :], ALU.add).then_inc(S["rotated"], 1)
                        v_.tensor_tensor(kall[:, CTX:TOK], rtmp[:, 1, :], rtmp2[:, 1, :], ALU.add).then_inc(S["rotated"], 1)
                        for k in range(4):
                            each("scores_done", 4, k + 1)
                            steps.link(v_.reduce_max(stat[:, k:k + 1], bank[:, 4 + k, :], AX_X))
                            v_.tensor_scalar(stat[:, 4 + k:5 + k], stat[:, k:k + 1], -HALF ** -0.5, None, ALU.mult
                                             ).then_inc(S["max_done"], 1)
                        for t in range(2):
                            each("probs_done", 4, 2 * t + 2)
                            steps.link(v_.reciprocal(stat[:, 12 + 2 * t:14 + 2 * t], stat[:, 8 + 2 * t:10 + 2 * t]))
                            steps.did(v_.tensor_scalar(stat[:, 16 + t:17 + t], stat[:, 13 + 2 * t:14 + 2 * t], lamv[:, 5:6], None, ALU.mult))
                            steps.link(v_.tensor_scalar(amix[:, t, :], probs[:, 2 * t, :], stat[:, 12 + 2 * t:13 + 2 * t], None, ALU.mult))
                            v_.scalar_tensor_tensor(amix[:, t, :], probs[:, 2 * t + 1, :], stat[:, 16 + t:17 + t], amix[:, t, :],
                                                    ALU.mult, ALU.add).then_inc(S["mixed_done"], 1)
                        each("attn_root", 1, 1)
                        steps.link(v_.reciprocal(rat, rat))
                        v_.scalar_tensor_tensor(big[:, ds(h + 3 * KC, 1), 0:LAT], oat.unsqueeze(1), lamv[:, 6:7], rat.unsqueeze(1),
                                                ALU.mult, ALU.mult).then_inc(S["head_closed"], 1)
                    go = g0 + 32

                steps.link(v_.memset(ssq[:, :], 0.0))

                def out_four(it, with_mod):
                    for r in range(4):
                        if with_mod and r > 0:
                            vec = it * 3 + (mod0[n] // KC + r - 1)
                            mod_rows(vec)
                            mod_columns(vec, 0 if mod0[n] // KC < 9 else 1)
                        dve.wait_ge(S["out_squared"], n * KC + it * 4 + r + 1)
                        dve.wait_ge(S["acc_freed"], go + it * 4 + r + 4)
                        v_.tensor_tensor(ssq[:, c0:TOK], ssq[:, c0:TOK], sq[:, r % 2, c0:TOK], ALU.add
                                         ).then_inc(S["acc_freed"], 1)

                n_mod = MOD_INSIDE.get(n, 0) // 24
                if n_mod:
                    with dve.Fori(0, n_mod) as it:
                        out_four(it, True)
                if n_mod < 2:
                    with dve.Fori(n_mod, 2) as it:
                        out_four(it, False)

                dve.wait_ge(S["post_root"], n + 1)
                steps.link(v_.reciprocal(root[:, c0:TOK], root[:, c0:TOK]))
                with steps.loop(KC // 2, 2) as i:
                    for r in range(2):
                        done = steps.did(v_.tensor_tensor(hs[:, ds(i * 2 + r, 1), c0:TOK], hs[:, ds(i * 2 + r, 1), c0:TOK],
                                                          root[:, c0:TOK].unsqueeze(1), ALU.mult))
                    dve.wait_ge(steps.sem, done)
                    for r in range(2):
                        for cols, v in seg(c0):
                            last = v_.scalar_tensor_tensor(xs[:, ds(i * 2 + r, 1), cols], hs[:, ds(i * 2 + r, 1), cols],
                                                           post_scale[:, n, v, ds(i * 2 + r, 1)], xs[:, ds(i * 2 + r, 1), cols],
                                                           ALU.mult, ALU.add)
                        last.then_inc(S["x_updated"], 1)


_INS = ["x", "c", "ctx", "c_ctx", "w_mod", "b_mod", "norm_pre", "norm_post", "ffn_w_in", "ffn_w_out",
        "gdn_w_in", "gdn_conv", "gdn_A_log", "gdn_dt_bias", "gdn_o_gain", "gdn_w_out",
        "diff_w_in", "diff_lambda", "diff_subln", "diff_w_out"]


def kernel(**inputs):
    import numpy as _np
    import concourse.bacc as _bacc
    from concourse import mybir as _mybir
    from concourse.bass_utils import run_bass_kernel_spmd as _run

    nc = _bacc.Bacc("TRN2", target_bir_lowering=False, num_devices=1)
    arrays, args = {}, []
    for name in _INS:
        a = _np.ascontiguousarray(inputs[name])
        arrays[f"in_{name}"] = a
        args.append(nc.dram_tensor(f"in_{name}", a.shape, _mybir.dt.from_np(a.dtype), kind="ExternalInput").ap())
    consts = _np.concatenate(list(constant_blocks().values()), axis=1)
    arrays["in_consts"] = consts
    args.append(nc.dram_tensor("in_consts", consts.shape, _mybir.dt.from_np(consts.dtype), kind="ExternalInput").ap())
    args.append(nc.dram_tensor("out_0", (1, LAT, D), _mybir.dt.float32, kind="ExternalOutput").ap())
    hybrid_backbone(nc, *args)
    r = _run(nc, [arrays], core_ids=[0])
    return r.results[0]["out_0"]
```

```python
import math
from contextlib import ExitStack, contextmanager

import numpy as np

import concourse.bass as bass
from concourse import mybir

F32 = mybir.dt.float32
ALU = mybir.AluOpType
ACT = mybir.ActivationFunctionType
AX_X = mybir.AxisListType.X
ds = bass.ds

P = 128
D = 1024
KC = D // P
LAT = 256
CTX = 256
TOK = CTX + LAT
DFF = 2816
FC = DFF // P
DEPTH = 2
NSUB = 3
HEADS = 8
TAPS = 5
PAD = TAPS // 2
GRID_W = 64
HALF = 64
NC = TOK // P
EPS = 1e-6
GDN_IN = 4 * D + 4 * HEADS
LAM_INIT = 0.8 - 0.6 * math.exp(-0.3)
LEVELS = [2, 4, 8, 16, 32, 64]
WALK = [[0, 1, 2, 3], [1, 0, 3, 2]]

N_SMALL = 9
SLOTS = 4
UNIT = FC * P
MSLOTS = 4
MVEC = DEPTH * NSUB * 3

ROWS = {"norms": 96, "conv": 3 * KC * TAPS, "b_mod0": 72, "b_mod1": 72, "cond": 18}

SUBS = [("ffn", 0, 0), ("gdn", 0, 1), ("ffn", 0, 2), ("ffn", 1, 0), ("diff", 1, 1), ("ffn", 1, 2)]
UNITS = {"ffn": FC + KC, "gdn": 16 + 1 + 4, "diff": 12 + 4}
GROUPS = {"ffn": 2 * FC + KC, "gdn": 4 * KC + 1 + KC, "diff": 2 * KC + 16 + KC}
MOD_FIRST = 16
MOD_GATE = 8
MOD_INSIDE = {0: 48, 2: 48, 3: 24}


def constant_blocks():
    i = np.arange(P)
    s, c = i[:, None], i[None, :]
    blocks = {"ident": (s == c), "ones": np.ones((P, P))}
    blocks["incl0"], blocks["incl1"] = s <= c, s >= c
    blocks["strict0"], blocks["strict1"] = s < c, s > c
    pair = (s // 2 == c // 2)
    blocks["pair0"] = -1.0 * (pair & (s < c))
    blocks["pair1"] = -1.0 * (pair & (s > c))
    for w in LEVELS:
        same = (s // (2 * w)) == (c // (2 * w))
        blocks[f"lev0_{w}"] = same & (s % (2 * w) >= w) & (c % (2 * w) < w)
        blocks[f"lev1_{w}"] = same & (s % (2 * w) < w) & (c % (2 * w) >= w)
    rot = np.zeros((P, P))
    for k in range(0, P, 2):
        rot[k + 1, k] = -1.0
        rot[k, k + 1] = 1.0
    blocks["rot"] = rot
    half = HALF // 2
    inv = (np.float32(10000.0) ** (-np.arange(0, half, 2, dtype=np.float32) / np.float32(half))).astype(np.float32)
    tok = np.arange(LAT)
    ang = np.concatenate([(tok // GRID_W).astype(np.float32)[:, None] * inv,
                          (tok % GRID_W).astype(np.float32)[:, None] * inv], axis=-1)
    feat = (i % HALF) // 2
    blocks["cos"] = np.cos(ang).T[feat]
    blocks["sin"] = np.sin(ang).T[feat]
    return {k: np.asarray(v, np.float32) for k, v in blocks.items()}


def constant_places():
    at, places = 0, {}
    for k, v in constant_blocks().items():
        places[k] = (at, v.shape[1])
        at += v.shape[1]
    return places, at


class Steps:

    def __init__(self, eng, sem):
        self.eng, self.sem, self.n, self.i, self.stride = eng, sem, 0, None, 0

    def did(self, ins):
        ins.then_inc(self.sem, 1)
        self.n += 1
        return self.n + self.i * self.stride if self.i is not None else self.n

    def link(self, ins):
        self.eng.wait_ge(self.sem, self.did(ins))

    @contextmanager
    def loop(self, count, stride):
        with self.eng.Fori(0, count) as i:
            before = self.n
            self.i, self.stride = i, stride
            yield i
            assert self.n - before == stride, (self.n - before, stride)
        self.i, self.n = None, before + count * stride


SEMAPHORES = """
 consts_landed rows_landed x_landed lam_landed unit_started mod_started
 rows_turned params_ready x_turned x_updated cond_ready banks_set pads_zeroed
 m_rows_done m_rows_copied m_turned m_ready
 acc_done acc_freed silu_done scales_ready
 out_squared post_sum post_root
 x_squared square_summed pre_root h_ready
 act_steps dve_steps
 conv_done
 ab_turned b_sigmoid a_abs a_exp g_ready G_summed G_exp head_closed
 qk_squared v_fixed pack_fixed qk_sums qk_roots qk_normed kv_turned grams decays_spread
 kv_copied exps_done tail_done qdec_done kdec_done diffs_done decays_done incl_done intra_done o_normed m2_done
 t_turned t_copied p1_done p1_masked ty_done ty_updated
 ks_done r_done v_done v_scaled o_done o_added s_done s_updated
 o_squared o_sum o_root
 lam_exp
 k_fixed turned_back rotated scores_done max_done probs_done mixed_done a_turned a_copied
 attn_done attn_squared attn_sum attn_root
 y_turned y_copied out_landed
""".split()



def hybrid_backbone(nc, x, c, ctx_in, c_ctx, w_mod, b_mod, norm_pre, norm_post, ffn_w_in, ffn_w_out,
                    gdn_w_in, gdn_conv, gdn_A_log, gdn_dt_bias, gdn_o_gain, gdn_w_out,
                    diff_w_in, diff_lambda, diff_subln, diff_w_out, consts, out):
    places, n_const = constant_places()
    unit0, group0, mod0 = [], [], {}
    u = g = 0
    m = MOD_FIRST + MOD_GATE
    for n, (kind, _, _) in enumerate(SUBS):
        unit0.append(u)
        group0.append(g)
        u += UNITS[kind]
        g += GROUPS[kind]
        if n in MOD_INSIDE:
            mod0[n] = m
            m += MOD_INSIDE[n]
    assert m == MVEC * KC
    ffns = [n for n, s in enumerate(SUBS) if s[0] == "ffn"]

    with ExitStack() as ctx:
        def sb(name, shape):
            return ctx.enter_context(nc.sbuf_tensor(name, shape, F32))

        S = {name: ctx.enter_context(nc.semaphore(name)) for name in SEMAPHORES}
        w_landed = [ctx.enter_context(nc.semaphore(f"w_landed{i}")) for i in range(SLOTS)]
        m_landed = [ctx.enter_context(nc.semaphore(f"m_landed{i}")) for i in range(MSLOTS)]

        bank = ctx.enter_context(nc.psum_tensor("bank", [P, 8, 512], F32))

        cst = sb("cst", [P, n_const])
        xs = sb("xs", [P, KC, TOK])
        hs = sb("hs", [P, KC, TOK])
        big = sb("big", [P, 4 * KC, TOK])
        ring = sb("ring", [P, SLOTS, UNIT])
        mring = sb("mring", [P, MSLOTS, D])
        prm = sb("prm", [P, len(ROWS), P])
        cond = sb("cond", [P, KC, 2])
        mrow = sb("mrow", [P, 256])
        modv = sb("modv", [P, MVEC, 2, KC])
        pre_scale = sb("pre_scale", [P, len(SUBS), 2, KC])
        post_scale = sb("post_scale", [P, len(SUBS), 2, KC])
        root = sb("root", [P, TOK])
        lamv = sb("lamv", [P, 8])
        pack_w = 5 * 2 * NC
        pack = sb("pack", [P, HEADS, pack_w])
        lam_row = sb("lam_row", [P, 4 * HALF])
        alog = sb("alog", [P, 2 * HEADS])
        dtb = sb("dtb", [P, 2 * HEADS])
        eps_col = sb("eps_col", [P, 4])
        ROOM = 7464
        room = sb("room", [P, ROOM])

        class Carver:

            def __init__(self, area, size):
                self.area, self.size, self.at = area, size, 0

            def __call__(self, *shape):
                ap = self.area[:, self.at:self.at + int(np.prod(shape))]
                self.at += int(np.prod(shape))
                assert self.at <= self.size, (self.at, self.size)
                if len(shape) == 2:
                    ap = ap.rearrange("p (a b) -> p a b", a=shape[0])
                return ap

        def k_(name):
            at, n = places[name]
            return cst[:, at:at + n]

        ident, ones = k_("ident"), k_("ones")
        flat_big = big[:, :, :].rearrange("p a b -> p (a b)")
        flat_hs = hs[:, :, :].rearrange("p a b -> p (a b)")

        carve = Carver(room, ROOM)
        sg = carve(2, TOK)
        sq = carve(2, TOK)
        ssq = carve(TOK)
        carve = Carver(room, ROOM)
        convp = carve(2, 2 * (LAT + 2 * PAD))
        conv_in = convp.rearrange("p a (s t) -> p a s t", s=2)
        convs = carve(2, TOK)
        ab = carve(TOK)
        gate_t = carve(7, NC * 2 * HEADS)
        carve = Carver(room, ROOM)
        qk_n = carve(2, TOK)
        vfix = carve(TOK)
        ktok = carve(TOK)
        ktail = carve(2, TOK)
        kdec = carve(2, TOK)
        qdec = carve(2, TOK)
        state = carve(2, P)
        r0 = carve(2, P)
        vnew = carve(2, P)
        osum = vfix
        vtok = [carve(TOK), ring[:, 0, KC * 256:KC * 256 + TOK]]
        hpack = [carve(pack_w), ring[:, 1, KC * 256:KC * 256 + pack_w]]
        orin = ring[:, 2, KC * 256:KC * 256 + TOK]
        carve = Carver(flat_hs, KC * TOK)
        expg = carve(2, TOK)
        m2t = carve(2, TOK)
        yy = carve(2, TOK)
        p1m = carve(2, TOK)
        carve = Carver(mring[:, :, :].rearrange("p a b -> p (a b)"), MSLOTS * D)
        sqk = carve(2, TOK)
        tt_ = carve(2, TOK)
        gt = carve(2, TOK)
        intra_odd = carve(2, TOK)
        carve = Carver(room, ROOM)
        carve(7464 - 1024)
        intra = [carve(2, TOK), intra_odd]
        carve = Carver(room, ROOM)
        qrot = carve(LAT)
        rtmp = carve(2, LAT)
        rtmp2 = carve(2, LAT)
        vhead = [carve(NC, P), carve(NC, P)]
        kall = [carve(TOK), carve(TOK)]
        amix = carve(2, TOK)
        at_ = carve(NC, LAT)
        stat = [carve(24), carve(24)]
        oat = carve(LAT)
        rat = carve(LAT)
        lam_prod = amix[:, 0, 0:2 * HALF].rearrange("p (a b) -> p a b", a=2)
        carve = Carver(flat_hs, KC * TOK)
        probs = [carve(4, TOK), carve(4, TOK)]
        v_rows = flat_big[:, 2 * KC * TOK:3 * KC * TOK].rearrange("p (t d) -> p t d", t=NC)

        def heads_of(loop, body):
            with loop(HEADS // 2 - 1) as it:
                for par in range(2):
                    body(it * 2 + par, par, True)
            body(HEADS - 2, 0, True)
            body(HEADS - 1, 1, False)

        def chunks(a):
            return a.rearrange("p (n e) -> p n e", n=NC)

        def per_token(f, d, par):
            return hpack[par][:, (f * 2 + d) * NC:(f * 2 + d + 1) * NC].unsqueeze(2).to_broadcast([P, NC, P])

        def col(f, d, t, par):
            return hpack[par][:, (f * 2 + d) * NC + t:(f * 2 + d) * NC + t + 1]

        rows_in = flat_big[:, 0:len(ROWS) * P].rearrange("p (a b) -> p a b", a=len(ROWS))
        x_in = flat_big[:, 1024:1024 + NC * D].rearrange("p (t d) -> p t d", t=NC)
        y_out = flat_big[:, 0:2 * D].rearrange("p (t d) -> p t d", t=2)
        names = list(ROWS)
        b_mod_col = [prm[:, names.index(f"b_mod{l}"), :] for l in range(DEPTH)]
        norms_col = prm[:, names.index("norms"), :]
        conv_col = prm[:, names.index("conv"), :]
        cond_col = prm[:, names.index("cond"), :]

        def lo(n):
            return CTX if n >= 4 else 0

        def pre_lo(n):
            return CTX if n > 4 else 0

        def seg(first):
            both = [(slice(0, CTX), 1), (slice(CTX, TOK), 0)]
            return both[1:] if first else both

        block = ctx.enter_context(nc.Block())

        def slot(s, k, width):
            return ring[:, s % SLOTS, 0:k * width].rearrange("p (k n) -> p k n", k=k)

        @block.sync
        def _(sp):
            sp.dma_start(cst[:, :], consts).then_inc(S["consts_landed"], 16)
            small = [
                (rows_in[0:48, 0, :], norm_pre.rearrange("l s (c p) -> (l s c) p", p=P)),
                (rows_in[48:96, 0, :], norm_post.rearrange("l s (c p) -> (l s c) p", p=P)),
                (rows_in[0:120, 1, :], gdn_conv.rearrange("o t (c p) -> (o t c) p", p=P)),
                (rows_in[0:72, 2, :], b_mod[0].rearrange("(c p) -> c p", p=P)),
                (rows_in[0:72, 3, :], b_mod[1].rearrange("(c p) -> c p", p=P)),
                (rows_in[0:8, 4, :], c.rearrange("o (c p) -> (o c) p", p=P)),
                (rows_in[8:16, 4, :], c_ctx.rearrange("(c p) -> c p", p=P)),
                (rows_in[16:17, 4, :], gdn_o_gain),
                (rows_in[17:18, 4, :], diff_subln),
            ]
            assert len(small) == N_SMALL
            for dst, src in small:
                sp.dma_start(dst, src).then_inc(S["rows_landed"], 16)
            sp.dma_start(x_in[:, 0:2, :], ctx_in[0].rearrange("(t p) d -> p t d", p=P)).then_inc(S["x_landed"], 16)
            sp.dma_start(x_in[:, 2:4, :], x[0].rearrange("(t p) d -> p t d", p=P)).then_inc(S["x_landed"], 16)
            for dst, src in ((alog[:, :], gdn_A_log), (dtb[:, :], gdn_dt_bias)):
                sp.dma_start(dst, src.rearrange("o d h -> o (d h)").to_broadcast([P, 2 * HEADS])
                             ).then_inc(S["lam_landed"], 16)
            sp.dma_start(lam_row[:, :], diff_lambda.rearrange("o a b -> o (a b)").to_broadcast([P, 4 * HALF])
                         ).then_inc(S["lam_landed"], 16)

            def load(w, unit, s, k, width, at, rows=P):
                sp.wait_ge(S["unit_started"], unit + 1)
                sp.dma_start(slot(s, k, width), w[:, ds(at, width)].rearrange("(k p) n -> p k n", p=rows)
                             ).then_inc(w_landed[s % SLOTS], 16)

            for n, (kind, l, j) in enumerate(SUBS):
                u = unit0[n]
                if kind == "ffn":
                    w_in, w_out = ffn_w_in[l, j // 2], ffn_w_out[l, j // 2]
                    with sp.Fori(0, FC // 4) as it:
                        for r in range(4):
                            load(w_in, u + it * 4 + r, u + r, KC, 256, it * 512 + (r // 2) * 256 + (r % 2) * DFF)
                    last = FC // 4 * 4
                    for r in range(2):
                        load(w_in, u + last + r, u + last + r, KC, 256, (FC - 2) * P + r * DFF)
                    uo = u + FC
                    with sp.Fori(0, KC // 4) as it:
                        for r in range(4):
                            load(w_out, uo + it * 4 + r, uo + r, FC, P, it * 512 + r * P)
                else:
                    w_in, w_out = (gdn_w_in[0], gdn_w_out[0]) if kind == "gdn" else (diff_w_in[0], diff_w_out[0])
                    trips = 4 if kind == "gdn" else 3
                    with sp.Fori(0, trips) as it:
                        for r in range(4):
                            load(w_in, u + it * 4 + r, u + r, KC, 256, it * 1024 + r * 256)
                    uo = u + 4 * trips
                    if kind == "gdn":
                        load(w_in, uo, uo, KC, 4 * HEADS, 4 * D)
                        uo += 1
                    for r in range(4):
                        load(w_out, uo + r, uo + r, KC, 256, r * 256)

            sp.wait_ge(S["y_copied"], KC)
            sp.dma_start(out[0].rearrange("(t p) d -> p t d", p=P), y_out).then_inc(S["out_landed"], 16)
            sp.wait_ge(S["out_landed"], 16)

        @block.gpsimd
        def _(pool):
            def mod_loads(l):
                with pool.Fori(0, 9) as v:
                    for k in range(KC):
                        pool.wait_ge(S["mod_started"], l * 9 * KC + v * KC + k + 1)
                        pool.dma_start(mring[:, k % MSLOTS, :], w_mod[l, k * P:(k + 1) * P, ds(v * D, D)]
                                       ).then_inc(m_landed[k % MSLOTS], 16)

            mod_loads(0)

            def of(sem, n, per, k):
                pool.wait_ge(S[sem], n * per + k)

            def v_fix(n):
                nc.gpsimd.tensor_copy(vfix, big[:, ds(n + 2 * KC, 1), :]).then_inc(S["v_fixed"], 1)

            def incl_decays(n, par):
                for d in range(2):
                    of("decays_done", n, 2, d + 1)
                    nc.gpsimd.tensor_tensor(chunks(intra[par][:, d, :]), chunks(gt[:, d, :]),
                                            k_(f"incl{d}").unsqueeze(1).to_broadcast([P, NC, P]), ALU.mult
                                            ).then_inc(S["incl_done"], 1)

            def decayed_qk(n):
                of("t_turned", n, 2, 2)
                of("exps_done", n, 2, 2)
                for d in range(2):
                    nc.gpsimd.tensor_tensor(qdec[:, d, :], qk_n[:, 1, :], expg[:, d, :], ALU.mult).then_inc(S["qdec_done"], 1)
                for d in range(2):
                    nc.gpsimd.tensor_tensor(kdec[:, d, :], qk_n[:, 0, :], expg[:, d, :], ALU.mult).then_inc(S["kdec_done"], 1)

            def one_head(h, par, more):
                of("kv_copied", h, 2, 2)
                of("pack_fixed", h, 1, 1)
                for d in range(2):
                    nc.gpsimd.tensor_tensor(chunks(ktail[:, d, :]), chunks(ktok), per_token(4, d, par),
                                            ALU.mult).then_inc(S["tail_done"], 1)
                if more:
                    of("head_closed", h, 1, 1)
                    v_fix(h + 1)
                    incl_decays(h + 1, 1 - par)
                    decayed_qk(h + 1)
                of("o_root", h, 1, 1)
                nc.gpsimd.tensor_tensor(osum, osum, orin, ALU.mult).then_inc(S["o_normed"], 1)
                of("o_normed", h, 1, 1)
                nc.gpsimd.tensor_tensor(big[:, ds(h + 2 * KC, 1), :], osum.unsqueeze(1), big[:, ds(h + 3 * KC, 1), :], ALU.mult
                                        ).then_inc(S["head_closed"], 1)

            pool.wait_ge(S["head_closed"], 1)
            v_fix(0)
            incl_decays(0, 0)
            decayed_qk(0)
            heads_of(lambda n: pool.Fori(0, n), one_head)
            pool.wait_ge(S["head_closed"], HEADS + 1)
            mod_loads(1)

            def kv_fix(n, par):
                nc.gpsimd.tensor_copy(kall[par][:, 0:CTX].unsqueeze(1), big[:, ds(n + KC, 1), 0:CTX]).then_inc(S["k_fixed"], 1)
                nc.gpsimd.tensor_copy(vhead[par], v_rows[:, :, ds(n * P, P)]).then_inc(S["v_fixed"], 1)

            def head_leaves(n):
                of("attn_root", n, 1, 1)
                nc.gpsimd.tensor_tensor(big[:, ds(n + 3 * KC, 1), 0:LAT], oat.unsqueeze(1), rat.unsqueeze(1), ALU.mult
                                        ).then_inc(S["head_closed"], 1)

            pool.wait_ge(S["head_closed"], HEADS + 2)
            kv_fix(0, 0)
            kv_fix(1, 1)
            with pool.Fori(0, HEADS // 2 - 1) as it:
                for par in range(2):
                    head_leaves(it * 2 + par)
                    kv_fix(it * 2 + (par + 2), par)
            head_leaves(HEADS - 2)
            head_leaves(HEADS - 1)

        @block.tensor
        def _(pe):
            mm = nc.tensor.matmul
            turn = nc.tensor.transpose

            pe.wait_ge(S["consts_landed"], 16)
            pe.wait_ge(S["rows_landed"], N_SMALL * 16)
            for b, rows in enumerate(ROWS.values()):
                turn(bank[:, b, 0:rows], rows_in[0:rows, b, :], ident[0:rows, 0:rows]).then_inc(S["rows_turned"], 1)
            pe.wait_ge(S["x_landed"], 32)
            for k in range(KC):
                b = (5 + k) % 8
                if k >= 3:
                    pe.wait_ge(S["params_ready"], k - 2)
                for t in range(NC):
                    last = turn(bank[:, b, t * P:(t + 1) * P], x_in[:, t, k * P:(k + 1) * P], ident)
                last.then_inc(S["x_turned"], 1)

            def mod_unit(i, k):
                pe.wait_ge(m_landed[k % MSLOTS], i * (KC * 16 // MSLOTS) + (k // MSLOTS + 1) * 16)
                if k == 0:
                    pe.wait_ge(S["m_rows_copied"], i + 1)
                for q in range(4):
                    last = mm(bank[32 * q:32 * q + 2, 4, 0:256], cond[:, k, :],
                              mring[:, k % MSLOTS, q * 256:(q + 1) * 256], start=(k == 0), stop=(k == KC - 1))
                    if q == 0:
                        last.then_inc(S["mod_started"], 1)
                if k == KC - 1:
                    last.then_inc(S["m_rows_done"], 1)

            def mod_turn(i):
                pe.wait_ge(S["m_rows_copied"], i + 2)
                turn(bank[:, 5, 0:P], mrow[:, 0:P], ident)
                turn(bank[:, 5, P:2 * P], mrow[:, P:2 * P], ident).then_inc(S["m_turned"], 1)

            def unit_wait(unit, s):
                s %= SLOTS
                pe.wait_ge(w_landed[s], (unit - s) * (16 // SLOTS) + 16)

            def group(g, r, w, rhs, cols=TOK, rows=P, starts=False, ready=None):
                pe.wait_ge(S["acc_freed"], g + 1)
                n_k = w.shape[1]
                for k in range(n_k):
                    if ready is not None:
                        ready(k)
                    last = mm(bank[0:rows, r % 4, 0:cols], w[:, k, :], rhs(k), start=(k == 0), stop=(k == n_k - 1))
                    if k == 0 and starts:
                        last.then_inc(S["unit_started"], 1)
                last.then_inc(S["acc_done"], 1)

            pe.wait_ge(S["cond_ready"], 1)
            pe.wait_ge(S["x_updated"], KC)
            with pe.Fori(0, MOD_FIRST // KC) as i:
                for k in range(KC):
                    mod_unit(i, k)
                mod_turn(i)

            for n, (kind, l, j) in enumerate(SUBS):
                u0, g0, c0, p0 = unit0[n], group0[n], lo(n), pre_lo(n)
                for k in range(KC):
                    pe.wait_ge(S["x_squared"], n * KC + k + 1)
                    mm(bank[:, 7, p0:TOK], ones, sq[:, k % 2, p0:TOK], start=(k == 0), stop=(k == KC - 1)
                       ).then_inc(S["square_summed"], 1)

                def h_wait(k, n=n):
                    pe.wait_ge(S["h_ready"], n * KC + k + 1)

                if kind == "ffn":
                    def pair(i, a, fresh=False, with_mod=False):
                        for v in range(2):
                            s = u0 + a + v
                            unit_wait(u0 + i * 2 + v, s)
                            for jj in range(2):
                                pe.wait_ge(S["acc_freed"], g0 + i * 4 + (4 if jj else 2))
                                w = slot(s, KC, 256)
                                for k in range(KC):
                                    if fresh and v == 0 and jj == 0:
                                        h_wait(k)
                                    last = mm(bank[:, (g0 + 2 * v + jj) % 4, 0:TOK - c0], w[:, k, jj * P:(jj + 1) * P],
                                              hs[:, k, c0:TOK], start=(k == 0), stop=(k == KC - 1))
                                    if k == 0 and jj == 0:
                                        last.then_inc(S["unit_started"], 1)
                                    if with_mod and k % 4 == 2:
                                        mod_unit(MOD_FIRST // KC, 4 * v + 2 * jj + k // 4)
                                last.then_inc(S["acc_done"], 1)

                    with pe.Fori(0, FC // 4) as it:
                        pair(it * 2, 0, fresh=True)
                        pair(it * 2 + 1, 2)
                    pair(FC // 2 - 1, FC // 4 * 4, with_mod=(n == 0))
                    if n == 0:
                        mod_turn(MOD_FIRST // KC)

                    uo, go = u0 + FC, g0 + 2 * FC

                    def hidden_wait(k):
                        if k == 0:
                            pe.wait_ge(S["acc_freed"], go)
                        elif k >= FC - 2:
                            pe.wait_ge(S["acc_freed"], go + 2 * (k - (FC - 2)) + 2)

                    def out_four(it, with_mod):
                        for r in range(4):
                            def between(k, r=r):
                                hidden_wait(k)
                                if with_mod and k % 3 == 2 and k < 18:
                                    m = 6 * r + k // 3
                                    mod_unit(it * 3 + (mod0[n] // KC + m // KC), m % KC)
                            unit_wait(uo + it * 4 + r, uo + r)
                            group(go + it * 4 + r, go + r, slot(uo + r, FC, P), lambda k: big[:, k, 0:TOK - c0],
                                  cols=TOK - c0, starts=True, ready=between)
                            if with_mod and r > 0:
                                mod_turn(it * 3 + (mod0[n] // KC + r - 1))

                    n_mod = MOD_INSIDE.get(n, 0) // 24
                    if n_mod:
                        with pe.Fori(0, n_mod) as it:
                            out_four(it, True)
                    if n_mod < 2:
                        with pe.Fori(n_mod, 2) as it:
                            out_four(it, False)

                if kind == "gdn":
                    with pe.Fori(0, 4) as it:
                        for r in range(4):
                            unit_wait(u0 + it * 4 + r, u0 + r)
                            for jj in range(2):
                                q = 2 * r + jj
                                group(g0 + it * 8 + q, g0 + q, slot(u0 + r, KC, 256)[:, :, jj * P:(jj + 1) * P],
                                      lambda k: hs[:, k, :], starts=(jj == 0), ready=h_wait if q == 0 else None)
                    ua, ga = u0 + 16, g0 + 32
                    unit_wait(ua, ua)
                    group(ga, ga, slot(ua, KC, 4 * HEADS), lambda k: hs[:, k, :], rows=4 * HEADS, starts=True)
                    pe.wait_ge(S["acc_freed"], ga + 1 + 4)
                    for t in range(NC):
                        last = turn(bank[:, 4, t * 32:(t + 1) * 32], ab[0:32, t * P:(t + 1) * P], ident[0:32, 0:32])
                    last.then_inc(S["ab_turned"], 1)
                    pe.wait_ge(S["g_ready"], 1)
                    for d in range(2):
                        mm(bank[:, 5, d * 32:(d + 1) * 32].rearrange("p (n h) -> p n h", n=NC), k_(f"incl{d}"),
                           gate_t[:, 2, :].rearrange("p (n h) -> p n h", n=NC)[:, :, d * HEADS:(d + 1) * HEADS],
                           start=True, stop=True)
                    mm(bank[:, 6, 0:64], ones, gate_t[:, 2, :], start=True, stop=True).then_inc(S["G_summed"], 1)

                    def of(sem, n, per, k):
                        pe.wait_ge(S[sem], n * per + k)

                    n_lev = len(LEVELS)
                    ch = [slice(t * P, (t + 1) * P) for t in range(NC)]

                    def qk_square_sums(n):
                        of("qk_squared", n, 2, 2)
                        for a in range(2):
                            last = mm(bank[:, 6 + a, :], ones, sqk[:, a, :], start=True, stop=True)
                        last.then_inc(S["qk_sums"], 1)

                    def spread_decays(n, par):
                        of("qk_roots", n, 2, 2)
                        of("pack_fixed", n, 1, 1)
                        for d in range(2):
                            for t in range(NC):
                                last = mm(bank[:, 6 + d, ch[t]], hpack[par][:, d * NC + t:d * NC + t + 1].to_broadcast([P, P]),
                                          k_(f"incl{d}"), start=True, stop=True)
                            last.then_inc(S["decays_spread"], 1)

                    def turn_kv(n):
                        of("diffs_done", n, 2, 2)
                        of("exps_done", n, 2, 2)
                        of("v_fixed", n, 1, 1)
                        for t in range(NC):
                            turn(bank[:, 6, ch[t]], vfix[:, ch[t]], ident)
                        of("qk_normed", n, 2, 2)
                        for t in range(NC):
                            last = turn(bank[:, 7, ch[t]], qk_n[:, 0, ch[t]], ident)
                        last.then_inc(S["kv_turned"], 1)

                    def grams(n):
                        of("kv_copied", n, 2, 2)
                        for t in range(NC):
                            last = mm(bank[:, 6 + t // 2, (t % 2) * 256:(t % 2) * 256 + 256].rearrange("p (a b) -> p a b", a=2),
                                      qk_n[:, 0, ch[t]], qk_n[:, :, ch[t]], start=True, stop=True)
                        last.then_inc(S["grams"], 1)

                    def first_t(n):
                        for d in range(2):
                            of("m2_done", n, 2, d + 1)
                            for t in range(NC):
                                last = turn(bank[:, 4 + d, ch[t]], gt[:, d, ch[t]], ident)
                            last.then_inc(S["t_turned"], 1)

                    def one_head(h, par, more):
                        for q, w in enumerate(LEVELS):
                            y = yy if q else gt
                            for d in range(2):
                                if q == 0:
                                    of("t_copied", h, 2, d + 1)
                                else:
                                    of("ty_updated", h, 2 * n_lev, 2 * (q - 1) + d + 1)
                                for t in range(NC):
                                    last = mm(bank[:, d, ch[t]], m2t[:, d, ch[t]], tt_[:, d, ch[t]], start=True, stop=True)
                                last.then_inc(S["p1_done"], 1)
                            if more and q == 0:
                                of("intra_done", h, 2, 2)
                                qk_square_sums(h + 1)
                            if more and q == 1:
                                spread_decays(h + 1, 1 - par)
                            if more and q == 4:
                                turn_kv(h + 1)
                            for d in range(2):
                                of("p1_masked", h, 2 * n_lev, 2 * q + d + 1)
                                if w != LEVELS[-1]:
                                    for t in range(NC):
                                        mm(bank[:, 2 + d, ch[t]], y[:, d, ch[t]], p1m[:, d, ch[t]], start=True, stop=True)
                                for t in range(NC):
                                    last = mm(bank[:, 4 + d, ch[t]], p1m[:, d, ch[t]], y[:, d, ch[t]], start=True, stop=True)
                                last.then_inc(S["ty_done"], 1)
                        of("kdec_done", h, 2, 2)
                        of("qdec_done", h, 2, 2)
                        of("tail_done", h, 2, 2)
                        for st in range(NC):
                            tc = [ch[WALK[d][st]] for d in range(2)]
                            for d in range(2):
                                if st:
                                    of("s_updated", h, 6, 2 * (st - 1) + d + 1)
                                    mm(bank[:, d, 0:P], kdec[:, d, tc[d]], state[:, d, :], start=True, stop=True
                                       ).then_inc(S["ks_done"], 1)
                            for d in range(2):
                                if st:
                                    of("r_done", h, 6, 2 * (st - 1) + d + 1)
                                else:
                                    of("ty_updated", h, 2 * n_lev, 2 * (n_lev - 1) + d + 1)
                                mm(bank[:, d, P:2 * P], yy[:, d, tc[d]], r0[:, d, :] if st else vtok[par][:, tc[d]],
                                   start=True, stop=True).then_inc(S["v_done"], 1)
                            if more and st == 0:
                                grams(h + 1)
                            for d in range(2):
                                if st:
                                    of("o_added", h, 8, 2 * (st - 1) + d + 1)
                                    mm(bank[:, 2 + d, 0:P], state[:, d, :], qdec[:, d, tc[d]], start=True, stop=False)
                                of("v_scaled", h, 8, 2 * st + d + 1)
                                if st < NC - 1:
                                    mm(bank[:, d, 2 * P:3 * P], ktail[:, d, tc[d]], vnew[:, d, :], start=True, stop=True
                                       ).then_inc(S["s_done"], 1)
                                if st == 0:
                                    of("intra_done", h, 2, 2)
                                mm(bank[:, 2 + d, 0:P], vnew[:, d, :], intra[par][:, d, tc[d]], start=(st == 0), stop=True
                                   ).then_inc(S["o_done"], 1)
                        if more:
                            first_t(h + 1)
                            of("intra_done", h + 1, 2, 2)
                        of("o_squared", h, 1, 1)
                        mm(bank[:, 6, :], ones, orin, start=True, stop=True).then_inc(S["o_sum"], 1)

                    pe.wait_ge(S["head_closed"], 1)
                    qk_square_sums(0)
                    spread_decays(0, 0)
                    turn_kv(0)
                    grams(0)
                    first_t(0)
                    heads_of(lambda n: pe.Fori(0, n), one_head)

                    pe.wait_ge(S["head_closed"], HEADS + 1)
                    uo, go = u0 + 17, g0 + 33
                    for r in range(4):
                        unit_wait(uo + r, uo + r)
                        for jj in range(2):
                            q = 2 * r + jj
                            group(go + q, go + q, slot(uo + r, KC, 256)[:, :, jj * P:(jj + 1) * P],
                                  lambda k: big[:, 2 * KC + k, :], starts=(jj == 0))

                if kind == "diff":
                    for part in range(2):
                        for r in range(4):
                            ux = u0 + part * 4 + r
                            unit_wait(ux, ux)
                            for jj in range(2):
                                g = g0 + part * 8 + 2 * r + jj
                                rhs = (lambda k: hs[:, k, CTX:TOK]) if part == 0 else (lambda k: hs[:, k, :])
                                group(g, g, slot(ux, KC, 256)[:, :, jj * P:(jj + 1) * P], rhs,
                                      cols=LAT if part == 0 else TOK, starts=(jj == 0), ready=h_wait if g == g0 else None)
                    for r in range(4):
                        ux = u0 + 8 + r
                        unit_wait(ux, ux)
                        for t in range(NC):
                            g = g0 + 16 + 4 * r + t
                            pe.wait_ge(S["acc_freed"], g + 1)
                            for k in range(KC):
                                last = mm(bank[:, g % 4, 0:256], hs[:, k, t * P:(t + 1) * P], slot(ux, KC, 256)[:, k, :],
                                          start=(k == 0), stop=(k == KC - 1))
                                if k == 0 and t == 0:
                                    last.then_inc(S["unit_started"], 1)
                            last.then_inc(S["acc_done"], 1)

                    def of(sem, n, per, k):
                        pe.wait_ge(S[sem], n * per + k)

                    def turn_back(n):
                        mm(bank[:, 0, 0:LAT].unsqueeze(1), k_("rot"), big[:, ds(n, 1), 0:LAT], start=True, stop=True)
                        mm(bank[:, 0, LAT:2 * LAT].unsqueeze(1), k_("rot"), big[:, ds(n + KC, 1), CTX:TOK],
                           start=True, stop=True).then_inc(S["turned_back"], 1)

                    def scores(n, par):
                        of("k_fixed", n, 1, 1)
                        of("rotated", n, 2, 2)
                        for t in range(2):
                            for m in range(2):
                                rows = slice(m * HALF, (m + 1) * HALF)
                                mm(bank[:, 4 + 2 * t + m, :], qrot[rows, t * P:(t + 1) * P], kall[par][rows, :], start=True, stop=True).then_inc(S["scores_done"], 1)

                    def one_head(h, par, more):
                        if more:
                            turn_back(h + 1)
                        for t in range(2):
                            of("mixed_done", h, 2, t + 1)
                            for kt in range(NC):
                                last = turn(bank[:, 2 + t, kt * P:(kt + 1) * P], amix[:, t, kt * P:(kt + 1) * P], ident)
                            last.then_inc(S["a_turned"], 1)
                        if more:
                            scores(h + 1, 1 - par)
                        of("a_copied", h, 2, 2)
                        pe.wait_ge(S["v_fixed"], h + (HEADS + 1))
                        for kt in range(NC):
                            last = mm(bank[:, 1, 0:LAT], vhead[par][:, kt, :], at_[:, kt, :], start=(kt == 0), stop=(kt == NC - 1))
                        last.then_inc(S["attn_done"], 1)
                        of("attn_squared", h, 1, 1)
                        mm(bank[:, 1, LAT:2 * LAT], ones, rat, start=True, stop=True).then_inc(S["attn_sum"], 1)

                    pe.wait_ge(S["head_closed"], HEADS + 2)
                    turn_back(0)
                    scores(0, 0)
                    heads_of(lambda n: pe.Fori(0, n), one_head)

                    pe.wait_ge(S["head_closed"], 2 * HEADS + 2)
                    uo, go = u0 + 12, g0 + 32
                    for r in range(4):
                        unit_wait(uo + r, uo + r)
                        for jj in range(2):
                            q = 2 * r + jj
                            group(go + q, go + q, slot(uo + r, KC, 256)[:, :, jj * P:(jj + 1) * P],
                                  lambda k: big[:, 3 * KC + k, 0:LAT], cols=LAT, starts=(jj == 0))

                pe.wait_ge(S["acc_freed"], group0[n] + GROUPS[kind] + 4)
                mm(bank[:, 6, c0:TOK], ones, ssq[:, c0:TOK], start=True, stop=True).then_inc(S["post_sum"], 1)

            for k in range(KC):
                pe.wait_ge(S["x_updated"], len(SUBS) * KC + k + 1)
                if k >= 4:
                    pe.wait_ge(S["y_copied"], k - 3)
                for t in range(2):
                    last = turn(bank[:, k % 4, t * P:(t + 1) * P], xs[:, k, CTX + t * P:CTX + (t + 1) * P], ident)
                last.then_inc(S["y_turned"], 1)

        @block.scalar
        def _(act):
            fn = nc.scalar.activation
            steps = Steps(act, S["act_steps"])

            def inv_root(dst, src, eps, scale):
                steps.link(fn(dst, src, ACT.Ln, bias=eps, scale=scale))
                return fn(dst, dst, ACT.Exp, scale=-0.5)

            act.wait_ge(S["params_ready"], len(ROWS))
            fn(cond[:, :, :].rearrange("p k v -> p v k"),
               cond_col[:, 0:16].rearrange("p (v k) -> p v k", v=2), ACT.Silu).then_inc(S["cond_ready"], 1)

            for n, (kind, l, j) in enumerate(SUBS):
                g0, c0, p0 = group0[n], lo(n), pre_lo(n)
                width = TOK - c0
                for k in range(KC):
                    act.wait_ge(S["x_updated"], n * KC + k + 1)
                    if k >= 2:
                        act.wait_ge(S["square_summed"], n * KC + k - 1)
                    fn(sq[:, k % 2, p0:TOK], xs[:, k, p0:TOK], ACT.Square).then_inc(S["x_squared"], 1)
                act.wait_ge(S["square_summed"], (n + 1) * KC)
                inv_root(root[:, p0:TOK], bank[:, 7, p0:TOK], eps_col[:, 0:1], 1.0 / D).then_inc(S["pre_root"], 1)

                if kind == "ffn":
                    jj0 = ffns.index(n) * FC

                    def gates(i, r):
                        for jj in range(2):
                            act.wait_ge(S["acc_done"], g0 + i * 4 + jj + 1)
                            act.wait_ge(S["acc_freed"], g0 + i * 4 + 2 * jj + 2)
                            fn(sg[:, jj, 0:width], bank[:, (g0 + jj) % 4, 0:width], ACT.Silu).then_inc(S["silu_done"], 1)

                    with act.Fori(0, FC // 2) as i:
                        gates(i, 0)
                    go = g0 + 2 * FC

                if kind == "gdn":
                    def conv_chunk(i, q):
                        g = g0 + i * 8 + q
                        act.wait_ge(S["acc_done"], g + 1)
                        fn(conv_in[:, q % 2, :, PAD:PAD + LAT], bank[:, (g0 + q) % 4, :].rearrange("p (s t) -> p s t", s=2),
                           ACT.Copy).then_inc(S["acc_freed"], 1)
                        act.wait_ge(S["conv_done"], i * 8 + q + 1)
                        steps.did(fn(big[:, ds(i * 8 + q, 1), :], convs[:, q % 2, :], ACT.Silu))

                    act.wait_ge(S["pads_zeroed"], 1)
                    with steps.loop(3, KC) as i:
                        for q in range(KC):
                            conv_chunk(i, q)
                    for q in range(KC):
                        g = g0 + 24 + q
                        act.wait_ge(S["acc_done"], g + 1)
                        fn(big[:, 3 * KC + q, :], bank[:, g % 4, :], ACT.Silu).then_inc(S["acc_freed"], 1)
                    g = g0 + 32
                    act.wait_ge(S["acc_done"], g + 1)
                    fn(ab[0:32, :], bank[0:32, g % 4, :], ACT.Copy).then_inc(S["acc_freed"], 1)
                    act.wait_ge(S["ab_turned"], 1)
                    act.wait_ge(S["a_abs"], 1)
                    fn(gate_t[:, 3, :].rearrange("p (n h) -> p n h", n=NC),
                       bank[:, 4, 0:P].rearrange("p (n h) -> p n h", n=NC)[:, :, 16:32], ACT.Sigmoid).then_inc(S["b_sigmoid"], 1)
                    steps.link(fn(gate_t[:, 1, :], gate_t[:, 1, :], ACT.Exp, scale=-1.0))
                    fn(gate_t[:, 1, :], gate_t[:, 1, :], ACT.Ln, bias=eps_col[:, 2:3])
                    fn(alog[:, :], alog[:, :], ACT.Exp).then_inc(S["a_exp"], 1)
                    act.wait_ge(S["G_exp"], 1)
                    fn(gate_t[:, 4, :], bank[:, 6, 0:64], ACT.Exp)
                    fn(gate_t[:, 5, :], gate_t[:, 5, :], ACT.Exp).then_inc(S["G_exp"], 1)

                    def of(sem, n, per, k):
                        act.wait_ge(S[sem], n * per + k)

                    def qk_squares(n):
                        for a in range(2):
                            fn(sqk[:, a, :].unsqueeze(1), big[:, ds(n + a * KC, 1), :], ACT.Square).then_inc(S["qk_squared"], 1)

                    def qk_roots(n):
                        of("qk_sums", n, 1, 1)
                        inv_root(sqk[:, 0, :], bank[:, 6, :], eps_col[:, 1:2], float(P)).then_inc(S["qk_roots"], 1)
                        inv_root(sqk[:, 1, :], bank[:, 7, :], eps_col[:, 0:1], 1.0).then_inc(S["qk_roots"], 1)

                    def exps(n):
                        for d in range(2):
                            of("decays_spread", n, 2, d + 1)
                            fn(expg[:, d, :], bank[:, 6 + d, :], ACT.Exp).then_inc(S["exps_done"], 1)

                    def decays(n, par):
                        for d in range(2):
                            of("diffs_done", n, 2, d + 1)
                            fn(gt[:, d, :], gt[:, d, :], ACT.Exp).then_inc(S["decays_done"], 1)
                        of("kv_turned", n, 1, 1)
                        fn(vtok[par], bank[:, 6, :], ACT.Copy).then_inc(S["kv_copied"], 1)
                        fn(ktok, bank[:, 7, :], ACT.Copy).then_inc(S["kv_copied"], 1)

                    def first_t(n):
                        for d in range(2):
                            of("t_turned", n, 2, d + 1)
                            fn(tt_[:, d, :], bank[:, 4 + d, :], ACT.Copy).then_inc(S["t_copied"], 1)

                    def one_head(h, par, more):
                        if more:
                            of("m2_done", h, 2, 2)
                            qk_squares(h + 1)
                            qk_roots(h + 1)
                            of("kdec_done", h, 2, 2)
                            of("tail_done", h, 2, 2)
                            exps(h + 1)
                            decays(h + 1, 1 - par)
                        for st in range(NC):
                            for d in range(2):
                                of("v_done", h, 8, 2 * st + d + 1)
                                if st:
                                    of("o_done", h, 8, 2 * (st - 1) + d + 1)
                                fn(vnew[:, d, :], bank[:, d, P:2 * P], ACT.Copy, scale=col(2, d, WALK[d][st], par)
                                   ).then_inc(S["v_scaled"], 1)
                        of("o_added", h, 8, 8)
                        of("head_closed", h, 1, 1)
                        fn(orin, osum, ACT.Square).then_inc(S["o_squared"], 1)
                        if more:
                            first_t(h + 1)
                        of("o_sum", h, 1, 1)
                        inv_root(orin, bank[:, 6, :], eps_col[:, 0:1], 1.0 / P).then_inc(S["o_root"], 1)

                    act.wait_ge(S["head_closed"], 1)
                    qk_squares(0)
                    qk_roots(0)
                    exps(0)
                    decays(0, 0)
                    first_t(0)

                    @contextmanager
                    def pairs(n):
                        with steps.loop(n, 2 * 3) as it:
                            yield it
                    heads_of(pairs, one_head)
                    go = g0 + 33

                if kind == "diff":
                    for q in range(KC):
                        g = g0 + q
                        act.wait_ge(S["acc_done"], g + 1)
                        fn(big[:, q, 0:LAT], bank[:, g % 4, 0:LAT], ACT.Copy).then_inc(S["acc_freed"], 1)
                    for q in range(KC):
                        g = g0 + KC + q
                        act.wait_ge(S["acc_done"], g + 1)
                        fn(big[:, KC + q, :], bank[:, g % 4, :], ACT.Copy).then_inc(S["acc_freed"], 1)
                    for r in range(4):
                        for t in range(NC):
                            g = g0 + 16 + 4 * r + t
                            act.wait_ge(S["acc_done"], g + 1)
                            fn(v_rows[:, t, r * 256:(r + 1) * 256], bank[:, g % 4, 0:256], ACT.Copy).then_inc(S["acc_freed"], 1)
                    act.wait_ge(S["lam_exp"], 1)
                    fn(lamv[:, 2:4], lamv[:, 0:2], ACT.Exp).then_inc(S["lam_exp"], 1)

                    def of(sem, n, per, k):
                        act.wait_ge(S[sem], n * per + k)

                    def exps(n, par):
                        for k in range(4):
                            of("max_done", n, 4, k + 1)
                            fn(probs[par][:, k, :], bank[:, 4 + k, :], ACT.Exp, bias=stat[par][:, 4 + k:5 + k], scale=HALF ** -0.5,
                               accum_out=stat[par][:, 8 + k:9 + k]).then_inc(S["probs_done"], 1)

                    def one_head(h, par, more):
                        for t in range(2):
                            of("a_turned", h, 2, t + 1)
                            fn(at_[:, :, t * P:(t + 1) * P], bank[:, 2 + t, :].rearrange("p (k q) -> p k q", k=NC),
                               ACT.Copy).then_inc(S["a_copied"], 1)
                        if more:
                            exps(h + 1, 1 - par)
                        of("attn_done", h, 1, 1)
                        act.wait_ge(S["head_closed"], h + (HEADS + 2))
                        fn(oat, bank[:, 1, 0:LAT], ACT.Copy, scale=lamv[:, 6:7])
                        fn(rat, bank[:, 1, 0:LAT], ACT.Square).then_inc(S["attn_squared"], 1)
                        of("attn_sum", h, 1, 1)
                        inv_root(rat, bank[:, 1, LAT:2 * LAT], eps_col[:, 0:1], 1.0 / P).then_inc(S["attn_root"], 1)

                    exps(0, 0)

                    @contextmanager
                    def pairs(n):
                        with steps.loop(n, 2) as it:
                            yield it
                    heads_of(pairs, one_head)
                    go = g0 + 32

                with act.Fori(0, 2) as i:
                    for r in range(4):
                        act.wait_ge(S["acc_done"], go + i * 4 + r + 1)
                        act.wait_ge(S["acc_freed"], go + i * 4 + r + 3)
                        acc = bank[:, (go + r) % 4, 0:width].unsqueeze(1)
                        fn(hs[:, ds(i * 4 + r, 1), c0:TOK], acc, ACT.Copy)
                        fn(sq[:, r % 2, c0:TOK].unsqueeze(1), acc, ACT.Square).then_inc(S["out_squared"], 1)
                act.wait_ge(S["post_sum"], n + 1)
                inv_root(root[:, c0:TOK], bank[:, 6, c0:TOK], eps_col[:, 0:1], 1.0 / D).then_inc(S["post_root"], 1)

            for k in range(KC):
                act.wait_ge(S["y_turned"], k + 1)
                fn(y_out[:, :, k * P:(k + 1) * P], bank[:, k % 4, 0:2 * P].rearrange("p (t f) -> p t f", t=2),
                   ACT.Copy).then_inc(S["y_copied"], 1)

        @block.vector
        def _(dve):
            v_ = nc.vector
            steps = Steps(dve, S["dve_steps"])

            v_.memset(eps_col[:, 0:1], EPS).then_inc(S["unit_started"], SLOTS - 1)
            v_.memset(eps_col[:, 1:2], EPS * P).then_inc(S["mod_started"], MSLOTS - 1)
            steps.did(v_.memset(eps_col[:, 2:3], 1.0))
            for b, rows in enumerate(ROWS.values()):
                dve.wait_ge(S["rows_turned"], b + 1)
                v_.tensor_copy(prm[:, b, 0:rows], bank[:, b, 0:rows]).then_inc(S["params_ready"], 1)
            for k in range(KC):
                dve.wait_ge(S["x_turned"], k + 1)
                v_.tensor_copy(xs[:, k, :], bank[:, (5 + k) % 8, :]).then_inc(S["x_updated"], 1)
            dve.wait_ge(S["x_updated"], KC)
            v_.memset(bank[:, 4, 0:256], 0.0).then_inc(S["m_rows_copied"], 1)
            v_.memset(lamv[:, 7:8], 0.0).then_inc(S["acc_freed"], 4)

            def mod_rows(i):
                dve.wait_ge(S["m_rows_done"], i + 1)
                v_.tensor_copy(mrow[:, :], bank[:, 4, 0:256]).then_inc(S["m_rows_copied"], 1)

            def mod_columns(i, l):
                dve.wait_ge(S["m_turned"], i + 1)
                turned = bank[:, 5, 0:256].rearrange("p (t q v) -> p v q t", t=2, q=4)[:, 0:2]
                bias = b_mod_col[l][:, ds((i - l * 9) * KC, KC)].rearrange("p (q t) -> p q t", t=2)
                for v in range(2):
                    last = v_.tensor_tensor(modv[:, ds(i, 1), v, :].rearrange("p o (q t) -> p (o q) t", t=2),
                                            turned[:, v], bias, ALU.add)
                last.then_inc(S["m_ready"], 1)

            with dve.Fori(0, MOD_FIRST // KC) as i:
                mod_rows(i)
                mod_columns(i, 0)

            for n, (kind, l, j) in enumerate(SUBS):
                g0, c0, p0 = group0[n], lo(n), pre_lo(n)
                width = TOK - c0
                m = l * 9 + j * 3
                dve.wait_ge(S["m_ready"], m + 2)
                at = l * 24 + j * KC
                scales = steps.did(v_.scalar_tensor_tensor(
                    pre_scale[:, n], modv[:, m + 1], 1.0,
                    norms_col[:, at:at + KC].unsqueeze(1).to_broadcast([P, 2, KC]), ALU.add, ALU.mult))

                dve.wait_ge(S["pre_root"], n + 1)
                dve.wait_ge(steps.sem, scales)
                with steps.loop(KC // 2, 2) as i:
                    for r in range(2):
                        done = steps.did(v_.tensor_tensor(hs[:, ds(i * 2 + r, 1), p0:TOK], xs[:, ds(i * 2 + r, 1), p0:TOK],
                                                          root[:, p0:TOK].unsqueeze(1), ALU.mult))
                    dve.wait_ge(steps.sem, done)
                    for r in range(2):
                        for cols, v in seg(p0):
                            last = v_.tensor_scalar(hs[:, ds(i * 2 + r, 1), cols], hs[:, ds(i * 2 + r, 1), cols],
                                                    pre_scale[:, n, v, ds(i * 2 + r, 1)], modv[:, m, v, ds(i * 2 + r, 1)],
                                                    ALU.mult, ALU.add)
                        last.then_inc(S["h_ready"], 1)

                if kind == "ffn":
                    s0 = ffns.index(n) * FC
                    with dve.Fori(0, FC // 2) as i:
                        for jj in range(2):
                            dve.wait_ge(S["acc_done"], g0 + i * 4 + jj + 3)
                            dve.wait_ge(S["silu_done"], s0 + i * 2 + jj + 1)
                            v_.tensor_tensor(big[:, ds(i * 2 + jj, 1), 0:width], bank[:, (g0 + 2 + jj) % 4, 0:width].unsqueeze(1),
                                             sg[:, jj, 0:width].unsqueeze(1), ALU.mult).then_inc(S["acc_freed"], 2)
                    if n == 0:
                        mod_rows(MOD_FIRST // KC)
                        mod_columns(MOD_FIRST // KC, 0)
                    go = g0 + 2 * FC

                if kind == "gdn":
                    v_.memset(convp, 0.0).then_inc(S["pads_zeroed"], 1)
                    with steps.loop(3, KC * (TAPS - 1)) as i:
                        for q in range(KC):
                            dve.wait_ge(S["acc_freed"], g0 + 4 + i * KC + q + 1)
                            o = convs[:, q % 2, :].rearrange("p (s t) -> p s t", s=2)

                            def tap(t, i=i, q=q):
                                return conv_col[:, ds(i * KC + (t * 3 * KC + q), 1)]
                            steps.link(v_.tensor_scalar(o, conv_in[:, q % 2, :, 0:LAT], tap(0), None, ALU.mult))
                            for t in range(1, TAPS):
                                last = v_.scalar_tensor_tensor(o, conv_in[:, q % 2, :, t:t + LAT], tap(t), o, ALU.mult, ALU.add)
                                if t < TAPS - 1:
                                    steps.link(last)
                            last.then_inc(S["conv_done"], 1)

                    for q in range(KC):
                        dve.wait_ge(S["acc_freed"], g0 + 24 + q + 1 + 4)
                        v_.tensor_scalar(big[:, 3 * KC + q, :], big[:, 3 * KC + q, :], cond_col[:, 16:17], None, ALU.mult)

                    def by_token(a):
                        return gate_t[:, a, :].rearrange("p (n h) -> p n h", n=NC)

                    def over_tokens(a):
                        return a.unsqueeze(1).to_broadcast([P, NC, 2 * HEADS])

                    dve.wait_ge(S["ab_turned"], 1)
                    dve.wait_ge(S["lam_landed"], 48)
                    steps.link(v_.tensor_tensor(by_token(0), bank[:, 4, 0:P].rearrange("p (n h) -> p n h", n=NC)[:, :, 0:16],
                                                over_tokens(dtb[:, :]), ALU.add))
                    v_.scalar_tensor_tensor(gate_t[:, 1, :], gate_t[:, 0, :], -1.0, gate_t[:, 0, :], ALU.mult, ALU.max
                                            ).then_inc(S["a_abs"], 1)
                    steps.link(v_.tensor_scalar(gate_t[:, 6, :], gate_t[:, 0, :], 0.0, None, ALU.max))
                    dve.wait_ge(S["a_exp"], 1)
                    steps.link(v_.tensor_tensor(gate_t[:, 0, :], gate_t[:, 6, :], gate_t[:, 1, :], ALU.add))
                    v_.scalar_tensor_tensor(by_token(2), by_token(0), -1.0, over_tokens(alog[:, :]), ALU.mult, ALU.mult
                                            ).then_inc(S["g_ready"], 1)
                    dve.wait_ge(S["G_summed"], 1)
                    steps.link(v_.tensor_copy(gate_t[:, 6, :].rearrange("p (n d h) -> p d n h", n=NC, d=2),
                                              bank[:, 5, 0:64].rearrange("p (d n h) -> p d n h", d=2, n=NC)))
                    v_.tensor_tensor(gate_t[:, 5, :], bank[:, 6, 0:64], gate_t[:, 6, :], ALU.subtract).then_inc(S["G_exp"], 1)
                    dve.wait_ge(S["b_sigmoid"], 1)
                    dve.wait_ge(S["G_exp"], 2)
                    for f, src in enumerate((2, 6, 3, 4, 5)):
                        for d in range(2):
                            last = v_.tensor_copy(pack[:, :, (f * 2 + d) * NC:(f * 2 + d + 1) * NC],
                                                  gate_t[:, src, :].rearrange("p (n d h) -> p d h n", n=NC, d=2)[:, d])
                    last.then_inc(S["head_closed"], 1)

                    def of(sem, n, per, k):
                        dve.wait_ge(S[sem], n * per + k)

                    def over_chunks(name):
                        return k_(name).unsqueeze(1).to_broadcast([P, NC, P])

                    gram = bank[:, 6:8, :].rearrange("p b f -> p (b f)").rearrange("p (t a c) -> p t a c", t=NC, a=2)
                    n_lev = len(LEVELS)
                    taken = {}

                    def fix_pack(n, par):
                        v_.tensor_copy(hpack[par].unsqueeze(1), pack[:, ds(n, 1), :]).then_inc(S["pack_fixed"], 1)

                    def norm_qk(n):
                        of("qk_roots", n, 2, 2)
                        v_.tensor_tensor(qk_n[:, 1, :].unsqueeze(1), big[:, ds(n, 1), :], sqk[:, 0, :].unsqueeze(1), ALU.mult
                                         ).then_inc(S["qk_normed"], 1)
                        v_.tensor_tensor(qk_n[:, 0, :].unsqueeze(1), big[:, ds(n + KC, 1), :], sqk[:, 1, :].unsqueeze(1), ALU.mult
                                         ).then_inc(S["qk_normed"], 1)

                    def subtract_g(n, par):
                        of("pack_fixed", n, 1, 1)
                        for d in range(2):
                            of("exps_done", n, 2, d + 1)
                            taken["g", d] = steps.did(v_.tensor_tensor(chunks(gt[:, d, :]), chunks(bank[:, 6 + d, :]),
                                                                       per_token(1, d, par), ALU.subtract))

                    def bound_g():
                        for d in range(2):
                            dve.wait_ge(steps.sem, taken["g", d])
                            v_.tensor_scalar(gt[:, d, :], gt[:, d, :], 0.0, None, ALU.min).then_inc(S["diffs_done"], 1)

                    def strict_decays(n):
                        of("qk_normed", n, 2, 2)
                        for d in range(2):
                            of("decays_done", n, 2, d + 1)
                            taken["strict", d] = steps.did(v_.tensor_tensor(chunks(sqk[:, d, :]), chunks(gt[:, d, :]),
                                                                            over_chunks(f"strict{d}"), ALU.mult))

                    def times_beta(par):
                        for d in range(2):
                            dve.wait_ge(steps.sem, taken["strict", d])
                            taken["beta", d] = steps.did(v_.tensor_tensor(chunks(sqk[:, d, :]), chunks(sqk[:, d, :]),
                                                                          per_token(2, d, par), ALU.mult))

                    def make_m2(n):
                        of("grams", n, 1, 1)
                        for d in range(2):
                            dve.wait_ge(steps.sem, taken["beta", d])
                            taken["m2", d] = steps.did(v_.tensor_tensor(chunks(m2t[:, d, :]), gram[:, :, 0, :], chunks(sqk[:, d, :]), ALU.mult))

                    def pair_m2(n):
                        of("incl_done", n, 2, 2)
                        for d in range(2):
                            dve.wait_ge(steps.sem, taken["m2", d])
                            taken["pair", d] = steps.did(v_.tensor_tensor(chunks(gt[:, d, :]), chunks(m2t[:, d, :]),
                                                                          over_chunks(f"pair{d}"), ALU.mult))

                    def first_y():
                        for d in range(2):
                            dve.wait_ge(steps.sem, taken["pair", d])
                            v_.tensor_tensor(chunks(gt[:, d, :]), chunks(gt[:, d, :]), over_chunks("ident"), ALU.add
                                             ).then_inc(S["m2_done"], 1)

                    def make_intra(par):
                        for d in range(2):
                            v_.tensor_tensor(chunks(intra[par][:, d, :]), gram[:, :, 1, :], chunks(intra[par][:, d, :]), ALU.mult
                                             ).then_inc(S["intra_done"], 1)

                    def one_head(h, par, more):
                        if more:
                            fix_pack(h + 1, 1 - par)
                        for q, w in enumerate(LEVELS):
                            for d in range(2):
                                of("p1_done", h, 2 * n_lev, 2 * q + d + 1)
                                v_.tensor_tensor(chunks(p1m[:, d, :]), chunks(bank[:, d, :]), over_chunks(f"lev{d}_{w}"),
                                                 ALU.mult).then_inc(S["p1_masked"], 1)
                            if more and q == 1:
                                of("kdec_done", h, 2, 2)
                                norm_qk(h + 1)
                            if more and q == 2:
                                subtract_g(h + 1, 1 - par)
                            if more and q == 3:
                                bound_g()
                            if more and q == 4:
                                strict_decays(h + 1)
                            if more and q == 5:
                                times_beta(1 - par)
                            for d in range(2):
                                of("ty_done", h, 2 * n_lev, 2 * q + d + 1)
                                if w != LEVELS[-1]:
                                    v_.tensor_tensor(tt_[:, d, :], tt_[:, d, :], bank[:, 2 + d, :], ALU.subtract)
                                v_.tensor_tensor(yy[:, d, :], (yy if q else gt)[:, d, :], bank[:, 4 + d, :], ALU.subtract
                                                 ).then_inc(S["ty_updated"], 1)
                        of("head_closed", h, 1, 1)
                        for st in range(NC):
                            for d in range(2):
                                if st:
                                    t = WALK[d][st]
                                    of("ks_done", h, 6, 2 * (st - 1) + d + 1)
                                    v_.tensor_tensor(r0[:, d, :], vtok[par][:, t * P:(t + 1) * P], bank[:, d, 0:P], ALU.subtract
                                                     ).then_inc(S["r_done"], 1)
                            if st < NC - 1:
                                for d in range(2):
                                    of("s_done", h, 6, 2 * st + d + 1)
                                    if st == 0:
                                        last = v_.tensor_copy(state[:, d, :], bank[:, d, 2 * P:3 * P])
                                    else:
                                        of("s_updated", h, 6, 2 * (st - 1) + d + 1)
                                        last = v_.scalar_tensor_tensor(state[:, d, :], state[:, d, :], col(3, d, WALK[d][st], par),
                                                                       bank[:, d, 2 * P:3 * P], ALU.mult, ALU.add)
                                    last.then_inc(S["s_updated"], 1)
                            if more:
                                [lambda: make_m2(h + 1), lambda: pair_m2(h + 1), first_y, lambda: make_intra(1 - par)][st]()
                            if st % 2:
                                of("o_added", h, 8, 2 * st)
                            for d in range(2):
                                t = WALK[d][st]
                                of("o_done", h, 8, 2 * st + d + 1)
                                o = osum[:, t * P:(t + 1) * P]
                                if st % 2:
                                    last = v_.tensor_tensor(o, o, bank[:, 2 + d, 0:P], ALU.add)
                                else:
                                    last = v_.tensor_copy(o, bank[:, 2 + d, 0:P])
                                last.then_inc(S["o_added"], 1)

                    dve.wait_ge(S["head_closed"], 1)
                    fix_pack(0, 0)
                    norm_qk(0)
                    subtract_g(0, 0)
                    bound_g()
                    strict_decays(0)
                    times_beta(0)
                    make_m2(0)
                    pair_m2(0)
                    first_y()
                    make_intra(0)

                    @contextmanager
                    def pairs(n):
                        with steps.loop(n, 2 * 10) as it:
                            yield it
                    heads_of(pairs, one_head)
                    go = g0 + 33

                if kind == "diff":
                    lp = lam_row[:, :].rearrange("p (a b c) -> p a b c", a=2, b=2)
                    steps.link(v_.tensor_tensor(lam_prod[:, :, :], lp[:, :, 0, :], lp[:, :, 1, :], ALU.mult))
                    v_.tensor_reduce(lamv[:, 0:2], lam_prod[:, :, :], axis=AX_X, op=ALU.add).then_inc(S["lam_exp"], 1)
                    dve.wait_ge(S["lam_exp"], 2)
                    steps.link(v_.tensor_tensor(lamv[:, 4:5], lamv[:, 3:4], lamv[:, 2:3], ALU.subtract))
                    v_.tensor_scalar(lamv[:, 5:6], lamv[:, 4:5], -LAM_INIT, None, ALU.add)
                    v_.tensor_scalar(lamv[:, 6:7], cond_col[:, 17:18], 1.0 - LAM_INIT, None, ALU.mult
                                     ).then_inc(S["head_closed"], 1)

                    def of(sem, n, per, k):
                        dve.wait_ge(S[sem], n * per + k)

                    def rotary(n, par):
                        q, k = big[:, ds(n, 1), 0:LAT], big[:, ds(n + KC, 1), CTX:TOK]
                        steps.did(v_.tensor_tensor(rtmp[:, 0:1, :], q, k_("cos").unsqueeze(1), ALU.mult))
                        steps.did(v_.tensor_tensor(rtmp[:, 1:2, :], k, k_("cos").unsqueeze(1), ALU.mult))
                        of("turned_back", n, 1, 1)
                        steps.link(v_.tensor_tensor(rtmp2, bank[:, 0, :].rearrange("p (a b) -> p a b", a=2),
                                                    k_("sin").unsqueeze(1).to_broadcast([P, 2, LAT]), ALU.mult))
                        v_.tensor_tensor(qrot, rtmp[:, 0, :], rtmp2[:, 0, :], ALU.add).then_inc(S["rotated"], 1)
                        v_.tensor_tensor(kall[par][:, CTX:TOK], rtmp[:, 1, :], rtmp2[:, 1, :], ALU.add).then_inc(S["rotated"], 1)

                    def maxima(n, par):
                        for k in range(4):
                            of("scores_done", n, 4, k + 1)
                            steps.link(v_.reduce_max(stat[par][:, k:k + 1], bank[:, 4 + k, :], AX_X))
                            v_.tensor_scalar(stat[par][:, 4 + k:5 + k], stat[par][:, k:k + 1], -HALF ** -0.5, None, ALU.mult
                                             ).then_inc(S["max_done"], 1)

                    def one_head(h, par, more):
                        st, pr = stat[par], probs[par]
                        for t in range(2):
                            of("probs_done", h, 4, 2 * t + 2)
                            steps.link(v_.reciprocal(st[:, 12 + 2 * t:14 + 2 * t], st[:, 8 + 2 * t:10 + 2 * t]))
                            steps.did(v_.tensor_scalar(st[:, 16 + t:17 + t], st[:, 13 + 2 * t:14 + 2 * t], lamv[:, 5:6], None, ALU.mult))
                            steps.link(v_.tensor_scalar(amix[:, t, :], pr[:, 2 * t, :], st[:, 12 + 2 * t:13 + 2 * t], None, ALU.mult))
                            v_.scalar_tensor_tensor(amix[:, t, :], pr[:, 2 * t + 1, :], st[:, 16 + t:17 + t], amix[:, t, :],
                                                    ALU.mult, ALU.add).then_inc(S["mixed_done"], 1)
                        if more:
                            rotary(h + 1, 1 - par)
                            maxima(h + 1, 1 - par)

                    rotary(0, 0)
                    maxima(0, 0)

                    @contextmanager
                    def pairs(n):
                        with steps.loop(n, 2 * (2 * 3 + 3 + 4)) as it:
                            yield it
                    heads_of(pairs, one_head)
                    go = g0 + 32

                if kind != "ffn":
                    dve.wait_ge(S["head_closed"], HEADS + 1 if kind == "gdn" else 2 * HEADS + 2)
                steps.link(v_.memset(ssq[:, :], 0.0))

                def out_four(it, with_mod):
                    for r in range(4):
                        if with_mod and r > 0:
                            vec = it * 3 + (mod0[n] // KC + r - 1)
                            mod_rows(vec)
                            mod_columns(vec, 0 if mod0[n] // KC < 9 else 1)
                        dve.wait_ge(S["out_squared"], n * KC + it * 4 + r + 1)
                        dve.wait_ge(S["acc_freed"], go + it * 4 + r + 4)
                        v_.tensor_tensor(ssq[:, c0:TOK], ssq[:, c0:TOK], sq[:, r % 2, c0:TOK], ALU.add
                                         ).then_inc(S["acc_freed"], 1)

                n_mod = MOD_INSIDE.get(n, 0) // 24
                if n_mod:
                    with dve.Fori(0, n_mod) as it:
                        out_four(it, True)
                if n_mod < 2:
                    with dve.Fori(n_mod, 2) as it:
                        out_four(it, False)

                dve.wait_ge(S["m_ready"], m + 3)
                steps.link(v_.scalar_tensor_tensor(
                    post_scale[:, n], modv[:, m + 2], 0.5 if kind == "ffn" else 1.0,
                    norms_col[:, 48 + at:48 + at + KC].unsqueeze(1).to_broadcast([P, 2, KC]), ALU.mult, ALU.mult))
                dve.wait_ge(S["post_root"], n + 1)
                with steps.loop(KC // 2, 2) as i:
                    for r in range(2):
                        done = steps.did(v_.tensor_tensor(hs[:, ds(i * 2 + r, 1), c0:TOK], hs[:, ds(i * 2 + r, 1), c0:TOK],
                                                          root[:, c0:TOK].unsqueeze(1), ALU.mult))
                    dve.wait_ge(steps.sem, done)
                    for r in range(2):
                        for cols, v in seg(c0):
                            last = v_.scalar_tensor_tensor(xs[:, ds(i * 2 + r, 1), cols], hs[:, ds(i * 2 + r, 1), cols],
                                                           post_scale[:, n, v, ds(i * 2 + r, 1)], xs[:, ds(i * 2 + r, 1), cols],
                                                           ALU.mult, ALU.add)
                        last.then_inc(S["x_updated"], 1)


_INS = ["x", "c", "ctx", "c_ctx", "w_mod", "b_mod", "norm_pre", "norm_post", "ffn_w_in", "ffn_w_out",
        "gdn_w_in", "gdn_conv", "gdn_A_log", "gdn_dt_bias", "gdn_o_gain", "gdn_w_out",
        "diff_w_in", "diff_lambda", "diff_subln", "diff_w_out"]


def kernel(**inputs):
    import numpy as _np
    import concourse.bacc as _bacc
    from concourse import mybir as _mybir
    from concourse.bass_utils import run_bass_kernel_spmd as _run

    nc = _bacc.Bacc("TRN2", target_bir_lowering=False, num_devices=1)
    arrays, args = {}, []
    for name in _INS:
        a = _np.ascontiguousarray(inputs[name])
        arrays[f"in_{name}"] = a
        args.append(nc.dram_tensor(f"in_{name}", a.shape, _mybir.dt.from_np(a.dtype), kind="ExternalInput").ap())
    consts = _np.concatenate(list(constant_blocks().values()), axis=1)
    arrays["in_consts"] = consts
    args.append(nc.dram_tensor("in_consts", consts.shape, _mybir.dt.from_np(consts.dtype), kind="ExternalInput").ap())
    args.append(nc.dram_tensor("out_0", (1, LAT, D), _mybir.dt.float32, kind="ExternalOutput").ap())
    hybrid_backbone(nc, *args)
    r = _run(nc, [arrays], core_ids=[0])
    return r.results[0]["out_0"]
```
